# Optimizing a Trainium2 kernel written in Bass

```python
import jax, jax.numpy as jnp
from jax import lax
import numpy as np

D_MODEL = 1024
BATCH = 1
SEQ = 1024
DEPTH = 1
DEC_BATCH = 8
DEC_SEQ = 1
PAST_LEN = 8192
PAGE_SIZE = 128

CONV_DIM = D_MODEL // 2
CONV_WIDTH = 31
RET_HEADS = 4
RET_QK_DIM = 128
RET_V_DIM = 256
RET_QK_WIDTH = RET_HEADS * RET_QK_DIM
RET_V_WIDTH = RET_HEADS * RET_V_DIM
RET_CHUNK = 128
FFN_DIM = 4 * D_MODEL
ROPE_BASE = 10000.0
EPS = 1e-6
IN_SIZES = (CONV_DIM, CONV_DIM, RET_QK_WIDTH, RET_QK_WIDTH, RET_V_WIDTH, RET_V_WIDTH, D_MODEL, D_MODEL)
IN_COLS = sum(IN_SIZES)
IN_SPLITS = [int(s) for s in np.cumsum(IN_SIZES)[:-1]]

kernel_name = "gated_conformer_retention_decoder_step"

def rms_norm(x, w):
    xf = x.astype(jnp.float32)
    y = xf * lax.rsqrt(jnp.mean(xf * xf, axis=-1, keepdims=True) + EPS)
    return (y * w.astype(jnp.float32)).astype(x.dtype)

def layer_norm(x, w, b):
    xf = x.astype(jnp.float32)
    mu = jnp.mean(xf, axis=-1, keepdims=True)
    xc = xf - mu
    y = xc * lax.rsqrt(jnp.mean(xc * xc, axis=-1, keepdims=True) + EPS)
    return (y * w.astype(jnp.float32) + b.astype(jnp.float32)).astype(x.dtype)

def rotary(x, pos):
    half = x.shape[-1] // 2
    freqs = 1.0 / (ROPE_BASE ** jnp.linspace(0.0, 1.0, half, dtype=jnp.float32))
    ang = pos[:, None] * freqs[None, :]
    c = jnp.cos(ang)[None, :, None, :]
    s = jnp.sin(ang)[None, :, None, :]
    x1, x2 = x[..., :half], x[..., half:]
    return jnp.concatenate([x1 * c - x2 * s, x2 * c + x1 * s], axis=-1)

def log_gammas():
    return jnp.log1p(-jnp.exp2(-5.0 - jnp.arange(RET_HEADS, dtype=jnp.float32)))

def retention_chunk(S, q, k, v):
    C = q.shape[1]
    lg = log_gammas()
    idx = jnp.arange(C, dtype=jnp.float32)
    diff = idx[:, None] - idx[None, :]
    causal = diff >= 0
    expo = jnp.where(causal, diff, 0.0)
    decay = jnp.where(causal[None], jnp.exp(expo[None] * lg[:, None, None]), 0.0)
    scores = jnp.einsum('bihd,bjhd->bhij', q, k) * decay[None]
    intra = jnp.einsum('bhij,bjhe->bihe', scores, v)
    q_decay = jnp.exp((idx + 1.0)[:, None] * lg[None, :])
    cross = jnp.einsum('bihd,bhde->bihe', q, S) * q_decay[None, :, :, None]
    k_decay = jnp.exp((C - 1.0 - idx)[:, None] * lg[None, :])
    S_new = jnp.exp(C * lg)[None, :, None, None] * S + jnp.einsum(
        'bjhd,bjhe->bhde', k * k_decay[None, :, :, None], v)
    return S_new, intra + cross

def retention_scan(q, k, v, S0):
    B, T = q.shape[0], q.shape[1]
    chunk = RET_CHUNK if T % RET_CHUNK == 0 else T
    n = T // chunk

    def to_chunks(a):
        return jnp.moveaxis(a.reshape(B, n, chunk, a.shape[2], a.shape[3]), 1, 0)

    def step(S, qkv):
        qc, kc, vc = qkv
        return retention_chunk(S, qc, kc, vc)

    S_fin, o = lax.scan(step, S0, (to_chunks(q), to_chunks(k), to_chunks(v)))
    o = jnp.moveaxis(o, 0, 1).reshape(B, T, RET_HEADS, RET_V_DIM)
    return S_fin, o

def mixer(xn, conv_buf, ret_state, pos, w_in, w_dw, b_dw, conv_ln_w, conv_ln_b,
          w_conv_out, w_ret_out, w_o):
    B, T, _ = xn.shape
    proj = xn @ w_in
    a_val, a_gate, q, k, v, g, gate_a, gate_b = jnp.split(proj, IN_SPLITS, axis=-1)

    u = a_val * jax.nn.sigmoid(a_gate)
    full = jnp.concatenate([conv_buf.astype(u.dtype), u], axis=1)
    conv = lax.conv_general_dilated(
        full, w_dw[:, None, :], window_strides=(1,), padding='VALID',
        dimension_numbers=('NWC', 'WIO', 'NWC'), feature_group_count=CONV_DIM) + b_dw
    new_buf = full[:, full.shape[1] - (CONV_WIDTH - 1):]
    a_out = jax.nn.silu(layer_norm(conv, conv_ln_w, conv_ln_b)) @ w_conv_out

    qf = rotary(q.reshape(B, T, RET_HEADS, RET_QK_DIM).astype(jnp.float32), pos)
    kf = rotary(k.reshape(B, T, RET_HEADS, RET_QK_DIM).astype(jnp.float32), pos) * (RET_QK_DIM ** -0.5)
    vf = v.reshape(B, T, RET_HEADS, RET_V_DIM).astype(jnp.float32)
    S_new, o = retention_scan(qf, kf, vf, ret_state.astype(jnp.float32))
    o = o * lax.rsqrt(jnp.mean(o * o, axis=-1, keepdims=True) + EPS)
    o = o.reshape(B, T, RET_V_WIDTH).astype(xn.dtype)
    b_out = (jax.nn.silu(g) * o) @ w_ret_out

    merged = jax.nn.sigmoid(gate_a) * a_out + jax.nn.sigmoid(gate_b) * b_out
    return merged @ w_o, new_buf, S_new

def block(x, conv_buf, ret_state, pos, p):
    (n_mix_pre, n_mix_post, w_in, w_dw, b_dw, conv_ln_w, conv_ln_b, w_conv_out,
     w_ret_out, w_o, n_ffn_pre, n_ffn_post, w_up, w_down) = p
    m, new_buf, S_new = mixer(rms_norm(x, n_mix_pre), conv_buf, ret_state, pos, w_in, w_dw, b_dw,
                              conv_ln_w, conv_ln_b, w_conv_out, w_ret_out, w_o)
    h = x + rms_norm(m, n_mix_post)
    f = jnp.square(jax.nn.relu(rms_norm(h, n_ffn_pre) @ w_up)) @ w_down
    return h + rms_norm(f, n_ffn_post), new_buf, S_new

def setup_inputs(seed: int = 0) -> dict:
    key = jax.random.key(seed)
    ks = jax.random.split(key, 20)
    f32 = jnp.float32

    def nrm(k, shape, scale):
        return jax.random.normal(k, shape, f32) * scale

    def gain(k, n):
        return 1.0 + nrm(k, (DEPTH, n), 0.02)

    return {
        "x_prompt": nrm(ks[0], (BATCH, SEQ, D_MODEL), 1.0),
        "x_sample": nrm(ks[1], (DEC_BATCH, DEC_SEQ, D_MODEL), 1.0),
        "cache_conv": nrm(ks[2], (DEPTH, DEC_BATCH, CONV_WIDTH - 1, CONV_DIM), 0.5),
        "state_ret": nrm(ks[3], (DEPTH, DEC_BATCH, RET_HEADS, RET_QK_DIM, RET_V_DIM), 0.5),
        "norm_mix_pre": gain(ks[4], D_MODEL),
        "norm_mix_post": gain(ks[5], D_MODEL),
        "w_in": nrm(ks[6], (DEPTH, D_MODEL, IN_COLS), D_MODEL ** -0.5),
        "w_dw": nrm(ks[7], (DEPTH, CONV_WIDTH, CONV_DIM), CONV_WIDTH ** -0.5),
        "b_dw": nrm(ks[8], (DEPTH, CONV_DIM), 0.01),
        "conv_ln_w": gain(ks[9], CONV_DIM),
        "conv_ln_b": nrm(ks[10], (DEPTH, CONV_DIM), 0.01),
        "w_conv_out": nrm(ks[11], (DEPTH, CONV_DIM, D_MODEL), CONV_DIM ** -0.5),
        "w_ret_out": nrm(ks[12], (DEPTH, RET_V_WIDTH, D_MODEL), RET_V_WIDTH ** -0.5),
        "w_o": nrm(ks[13], (DEPTH, D_MODEL, D_MODEL), D_MODEL ** -0.5),
        "norm_ffn_pre": gain(ks[14], D_MODEL),
        "norm_ffn_post": gain(ks[15], D_MODEL),
        "w_ffn_up": nrm(ks[16], (DEPTH, D_MODEL, FFN_DIM), D_MODEL ** -0.5),
        "w_ffn_down": nrm(ks[17], (DEPTH, FFN_DIM, D_MODEL), FFN_DIM ** -0.5),
    }

def reference(x_prompt, x_sample, cache_conv, state_ret, norm_mix_pre, norm_mix_post, w_in,
              w_dw, b_dw, conv_ln_w, conv_ln_b, w_conv_out, w_ret_out, w_o, norm_ffn_pre,
              norm_ffn_post, w_ffn_up, w_ffn_down):
    B, T = x_prompt.shape[0], x_prompt.shape[1]
    Bs, Ts = x_sample.shape[0], x_sample.shape[1]
    pos_p = jnp.arange(T, dtype=jnp.float32)
    pos_s = PAST_LEN + jnp.arange(Ts, dtype=jnp.float32)
    zero_buf = jnp.zeros((B, CONV_WIDTH - 1, CONV_DIM), x_prompt.dtype)
    zero_S = jnp.zeros((B, RET_HEADS, RET_QK_DIM, RET_V_DIM), jnp.float32)

    xp, xs = x_prompt, x_sample
    conv_p, ret_p, conv_s, ret_s = [], [], [], []
    for l in range(DEPTH):
        p = (norm_mix_pre[l], norm_mix_post[l], w_in[l], w_dw[l], b_dw[l], conv_ln_w[l],
             conv_ln_b[l], w_conv_out[l], w_ret_out[l], w_o[l], norm_ffn_pre[l],
             norm_ffn_post[l], w_ffn_up[l], w_ffn_down[l])
        xp, cb, sp = block(xp, zero_buf, zero_S, pos_p, p)
        xs, cbs, ss = block(xs, cache_conv[l], state_ret[l], pos_s, p)
        conv_p.append(cb)
        ret_p.append(sp)
        conv_s.append(cbs)
        ret_s.append(ss)

    new_conv_prompt = jnp.stack(conv_p)
    new_ret_prompt = jnp.stack(ret_p)
    new_conv_sample = jnp.stack(conv_s)
    new_ret_sample = jnp.stack(ret_s)
    return (xp, xs, new_conv_prompt, new_ret_prompt, new_conv_sample, new_ret_sample)


_drawn_inputs = setup_inputs


def setup_inputs(seed=0):
    import zlib

    import numpy as np

    out = dict(_drawn_inputs(seed))
    spreads = {}
    factors = {'norm_mix_post': 3.626,
     'b_dw': 5.328,
     'conv_ln_w': 12.313,
     'conv_ln_b': 23.229,
     'norm_ffn_pre': 12.868,
     'norm_ffn_post': 17.837}
    for name, (base, spread) in spreads.items():
        noise = np.random.default_rng([zlib.crc32(name.encode()), seed]).standard_normal(out[name].shape)
        drawn = base * np.exp(spread * noise) if base else spread * noise
        out[name] = __import__('jax').numpy.asarray(drawn.astype(out[name].dtype))
    for name, factor in factors.items():
        out[name] = (out[name] * factor).astype(out[name].dtype)
    return out
```

```python
from contextlib import ExitStack

import numpy as np

import concourse.bass as bass
from concourse import mybir

F32 = mybir.dt.float32
F32R = mybir.dt.float32r
ALU = mybir.AluOpType
ACT = mybir.ActivationFunctionType

P = 128
D_MODEL = 1024
SEQ = 1024
DEC = 8
T = SEQ + DEC
CHUNKS = 3
CH = T // CHUNKS
KT = D_MODEL // P
CONV_DIM = 512
CT = CONV_DIM // P
TAPS = 31
HIST = TAPS - 1
UW = HIST + T
HEADS = 4
PAIRS = HEADS // 2
DK = 128
DV = 256
RC = 128
NRC = SEQ // RC
FFN = 4096
EPS = 1e-6
PAST_LEN = 8192
ROPE_BASE = 10000.0
GAMMA = [1.0 - 2.0 ** (-5.0 - h) for h in range(HEADS)]

SLOT_TILES = 4
SLOT = SLOT_TILES * P
FB = 2
NFB = FFN // P // FB
RAW = 4
HL = 2

V_PRE, V_POST, V_FPRE, V_FPOST, V_LNW, V_LNB, V_BDW, NVEC = 0, 8, 16, 24, 32, 36, 40, 44

G_XSTAT = 0
G_U, S_U = 1, 0
G_QKV, S_QKV = [9, 41], [16, 64]
G_G, S_G = [17, 49], [32, 80]
G_GA, S_GA = 21, 40
G_LNM, G_LNV = 23, 26
G_AOUT, S_AOUT = 31, 56
G_ON = [39, 53]
G_GB, S_GB = 55, 88
G_WO, S_WO = 71, 120
G_MSTAT = 79
G_FFN, S_FFN = 80, 136
G_FSTAT = 240
NSLOT = 264


def build(nc, xT, wseq, vecs, wdwT, cacheT, s_in, rope, mask_d, ident_d,
          yT, convp, convs, retp, rets):
    vscr = nc.dram_tensor("v_sample_scratch", (PAIRS, DEC, 2 * DV), F32, kind="Internal").ap()

    with ExitStack() as ctx:
        at = [16512]

        def place(name, shape, dt=F32, offset=None):
            n = 4 * int(np.prod(shape[1:]))
            off = at[0] if offset is None else offset
            if offset is None:
                at[0] += -(-n // 32) * 32
            return nc.alloc_sbuf_tensor_at(name, list(shape), dt, offset=off), off

        def sem(name):
            return ctx.enter_context(nc.semaphore(name))

        xn_h, a_A = place("xn_h", [P, KT, T], F32R)
        xn_l, a_B = place("xn_l", [P, KT, T], F32R)
        u_ext, a_C1 = place("u_ext", [P, CT, UW])
        conv, a_C2 = place("conv", [P, CT, T])
        x_in, a_D = place("x_in", [P, KT, T])
        a_D2 = a_D + 4 * CT * T
        ma, a_E = place("ma", [P, KT, T])
        a_E2 = a_E + 4 * CT * T
        gbuf, a_G = place("gbuf", [P, 4, T])
        raw, _ = place("raw", [P, RAW, SLOT])
        w_h, _ = place("w_h", [P, HL, SLOT], F32R)
        w_l, _ = place("w_l", [P, HL, SLOT], F32R)
        mg_h, _ = place("mg_h", [P, KT, T], F32R, a_A)
        mg_l, _ = place("mg_l", [P, KT, T], F32R, a_B)
        fx_h, _ = place("fx_h", [P, KT, T], F32R, a_A)
        fx_l, _ = place("fx_l", [P, KT, T], F32R, a_B)
        cv_h, _ = place("cv_h", [P, CT, UW], F32R, a_C1)
        cv_l, _ = place("cv_l", [P, CT, T], F32R, a_C2)
        qk1, _ = place("qk1", [P, 4, T], F32, a_C1)
        v1, _ = place("v1", [P, 4, T], F32, a_C2)
        ro1_h, _ = place("ro1_h", [P, 4, T], F32R, a_C1)
        ro1_l, _ = place("ro1_l", [P, 4, T], F32R, a_C2)
        x_again, _ = place("x_again", [P, KT, T], F32, a_C1)
        hid_h, _ = place("hid_h", [P, 2 * FB, T], F32R, a_C1)
        hid_l, _ = place("hid_l", [P, 2 * FB, T], F32R, a_C2)
        qk0, _ = place("qk0", [P, 4, T], F32, a_D)
        v0, _ = place("v0", [P, 4, T], F32, a_D2)
        ro0_h, _ = place("ro0_h", [P, 4, T], F32R, a_D)
        ro0_l, _ = place("ro0_l", [P, 4, T], F32R, a_D2)
        mix, _ = place("mix", [P, KT, T], F32, a_D)
        xsq, _ = place("xsq", [P, CHUNKS, KT * CH], F32, a_E)
        rope0, _ = place("rope0", [P, 4, T], F32, a_E)
        rtmp0, _ = place("rtmp0", [P, 4, CH], F32, a_E2)
        sgt, _ = place("sgt", [P, T], F32, a_G)
        hist, _ = place("hist", [P, CT, DEC, TAPS], F32, a_G + 4 * T)
        hprod, _ = place("hprod", [P, DEC, TAPS], F32, a_G + 8 * T)
        rope1, _ = place("rope1", [P, 4, T], F32, a_G)
        mask, _ = place("mask", [P, RC])
        ident, _ = place("ident", [P, P])
        ones, _ = place("ones", [P, P])
        vec, _ = place("vec", [P, NVEC])
        zero, _ = place("zero", [P, 1])
        eps_b, _ = place("eps_b", [P, 1])
        eps15_b, _ = place("eps15_b", [P, 1])
        kt_b, a_KT = place("kt_b", [P, 2, RC])
        vt_b, a_VT = place("vt_b", [P, 4, RC])
        p_b, _ = place("p_b", [P, 2, RC])
        state, _ = place("state", [P, 2, DV])
        s_dec, a_SS = place("s_dec", [P, 2, 2 * DV])
        v_bc, _ = place("v_bc", [P, 2 * DV])
        assert at[0] <= 229368, at[0]
        wdw, _ = place("wdw", [P, CT, TAPS], F32, a_VT)
        rtmp1, _ = place("rtmp1", [P, 4, CH], F32, a_SS)
        osq, _ = place("osq", [P, 2, 2 * CH], F32, a_SS)
        hsq, _ = place("hsq", [P, T], F32, a_KT)
        hsum, _ = place("hsum", [P, T], F32, a_SS)
        hms, _ = place("hms", [P, T], F32, a_SS)

        qk, vv = [qk0, qk1], [v0, v1]
        ro_h, ro_l = [ro0_h, ro1_h], [ro0_l, ro1_l]
        rtab, rtmp = [rope0, rope1], [rtmp0, rtmp1]

        ps = ctx.enter_context(nc.psum_tensor("ps", [P, 8, 512], F32))
        B6, B7 = ps[:, 6, :], ps[:, 7, :]

        def pset(g, n=CH):
            return ps[:, 3 * (g % 2):3 * (g % 2) + 3, 0:n]

        def pch(g, c):
            return ps[:, 3 * (g % 2) + c, 0:CH]

        def t3(ap):
            return ap.rearrange("p (c n) -> p c n", c=CHUNKS)

        x_ld = [sem(f"x_ld{c}") for c in range(CHUNKS)]
        cst_ld = sem("cst_ld")
        wdw_ld = sem("wdw_ld")
        hist_ld = sem("hist_ld")
        tab_ld = [sem("tab_ld0"), sem("tab_ld1")]
        raw_ld = [sem(f"raw_ld{i}") for i in range(RAW)]
        w_hi = sem("w_hi")
        w_split = sem("w_split")
        mm = sem("mm")
        ps_free = [sem("ps_free0"), sem("ps_free1")]
        c_init = sem("c_init")
        z_init = sem("z_init")
        x_sq = sem("x_sq")
        x_st = sem("x_st")
        x_ln = sem("x_ln")
        x_rs = sem("x_rs")
        x_sc = sem("x_sc")
        xn_hi = sem("xn_hi")
        xn_lo = sem("xn_lo")
        dve_c = sem("dve_c")
        cv_out = sem("cv_out")
        h_done = sem("h_done")
        cv_acc = sem("cv_acc")
        rope_p = sem("rope_p")
        rope_done = sem("rope_done")
        lnm_st = sem("lnm_st")
        lnv_st = sem("lnv_st")
        ln_xc = sem("ln_xc")
        ln_sq = sem("ln_sq")
        ln_ln = sem("ln_ln")
        ln_rs = sem("ln_rs")
        ln_n = sem("ln_n")
        ln_sg = sem("ln_sg")
        ln_z = sem("ln_z")
        ln_y = sem("ln_y")
        cv_hi = sem("cv_hi")
        cv_lo = sem("cv_lo")
        vs_T = sem("vs_T")
        vs_cp = sem("vs_cp")
        vs_st = sem("vs_st")
        staged = sem("staged")
        ret_a = sem("ret_a")
        vt_rdy = sem("vt_rdy")
        pk_rdy = sem("pk_rdy")
        ret_b = sem("ret_b")
        o_out = sem("o_out")
        s_upd = sem("s_upd")
        ss_ld = [sem("ss_ld0"), sem("ss_ld1")]
        ss_st = [sem("ss_st0"), sem("ss_st1")]
        vb_ld = sem("vb_ld")
        s_kv = sem("s_kv")
        s_new = sem("s_new")
        turns = sem("turns")
        g_sg = sem("g_sg")
        rp_st = sem("rp_st")
        on_sq = sem("on_sq")
        on_st = sem("on_st")
        on_ln = sem("on_ln")
        on_rs = sem("on_rs")
        on_n = sem("on_n")
        ro_g = sem("ro_g")
        ro_hi = sem("ro_hi")
        ro_lo = sem("ro_lo")
        mg_rdy = sem("mg_rdy")
        mg_hi = sem("mg_hi")
        mg_lo = sem("mg_lo")
        xa_ld = sem("xa_ld")
        wo_sq = sem("wo_sq")
        wo_sum = sem("wo_sum")
        m_st = sem("m_st")
        m_ln = sem("m_ln")
        m_rs = sem("m_rs")
        m_sc = sem("m_sc")
        h_dve = sem("h_dve")
        h_pool = sem("h_pool")
        fx_hi = sem("fx_hi")
        fx_lo = sem("fx_lo")
        hid_t = sem("hid_t")
        hid_hi = sem("hid_hi")
        hid_lo = sem("hid_lo")
        f_zero = sem("f_zero")
        h_sq = sem("h_sq")
        h_sum = sem("h_sum")
        h_st = sem("h_st")
        h_ms = sem("h_ms")
        f_den = sem("f_den")
        f_sq = sem("f_sq")
        f_sum = sem("f_sum")
        f_st = sem("f_st")
        f_ln = sem("f_ln")
        f_rs = sem("f_rs")
        y_sc = sem("y_sc")
        y_dve = sem("y_dve")
        y_pool = sem("y_pool")
        y_st = sem("y_st")

        def done(slot):
            return slot + 1 + HL

        E_FFN = done(S_FFN + 2 * FB - 1)
        PER_FB = 2 * FB + KT

        def taken(e, g, shift=0):
            e.wait_ge(ps_free[g % 2], shift + (g // 2 + 1))

        def free_set(pe, g, shift=0):
            if g >= 2:
                taken(pe, g - 2, shift)

        block = ctx.enter_context(nc.Block())

        @block.sync
        def _(sp):
            sp.dma_start(x_in[:, :, 0:CH], xT[:, :, 0:CH]).then_inc(x_ld[0], 16)
            for s in range(2):
                sp.dma_start(raw[:, s, :], wseq[s]).then_inc(raw_ld[s], 16)
            for c in (1, 2):
                sp.dma_start(x_in[:, :, c * CH:(c + 1) * CH], xT[:, :, c * CH:(c + 1) * CH]).then_inc(x_ld[c], 16)
            for s in range(2, RAW):
                sp.dma_start(raw[:, s, :], wseq[s]).then_inc(raw_ld[s], 16)
            with sp.Fori(1, NSLOT // RAW) as i:
                for s in range(RAW):
                    sp.wait_ge(w_split, i * RAW + (s - RAW + 1))
                    sp.dma_start(raw[:, s, :], wseq[bass.ds(i * RAW + s, 1)].rearrange("a p n -> (a p) n")
                                 ).then_inc(raw_ld[s], 16)
            for c in range(CHUNKS):
                cs = slice(c * CH, (c + 1) * CH)
                sp.wait_ge(y_dve, c + 1)
                sp.dma_start(yT[:, 0:4, cs], ma[:, 0:4, cs]).then_inc(y_st, 16)
                sp.wait_ge(y_pool, c + 1)
                sp.dma_start(yT[:, 4:8, cs], ma[:, 4:8, cs]).then_inc(y_st, 16)
            sp.wait_ge(y_st, 16 * CHUNKS * 2)
            sp.wait_ge(cv_out, 16 * 2)
            sp.wait_ge(rp_st, 16 * PAIRS)
            for s in range(2):
                sp.wait_ge(ss_st[s], 16 + 16 * (DEC // 2) * PAIRS)
            sp.wait_ge(vs_st, 16 * PAIRS)

        @block.gpsimd
        def _(pool):
            pool.memset(zero[:], 0.0).then_inc(z_init, 1)
            pool.wait_ge(z_init, 1)

            def split(s, n, loads, used):
                pool.wait_ge(raw_ld[s], loads)
                pool.wait_ge(mm, used)
                pool.tensor_tensor(w_h[:, s % HL, :], raw[:, s, :],
                                   zero[:, 0:1].broadcast_to([P, SLOT]), ALU.add).then_inc(w_hi, 1)
                pool.wait_ge(w_hi, n + 1)
                pool.tensor_tensor(w_l[:, s % HL, :], raw[:, s, :], w_h[:, s % HL, :].bitcast(F32),
                                   ALU.subtract).then_inc(w_split, 1)

            with pool.Fori(0, S_FFN // RAW) as i:
                for s in range(RAW):
                    split(s, i * RAW + s, i * 16 + 16, i * RAW + (s + 1))
            for s in range(RAW):
                n = S_FFN + s
                if s == HL:
                    pool.wait_ge(xa_ld, 16)
                    for c in range(CHUNKS):
                        cs = slice(c * CH, (c + 1) * CH)
                        pool.wait_ge(m_sc, c + 1)
                        pool.tensor_tensor(ma[:, 5:8, cs], mix[:, 5:8, cs], x_again[:, 5:8, cs], ALU.add
                                           ).then_inc(h_pool, 1)
                split(s, n, 16 * (n // RAW) + 16, n + 1)
            with pool.Fori(0, NFB - 1) as i:
                for j, used in enumerate((-1, 0, 1, 2, 3, 4, 6, 8)):
                    split(j % RAW, i * 8 + (S_FFN + 4 + j), i * 32 + 16 * ((S_FFN + 4 + j) // RAW + 1),
                          i * PER_FB + (E_FFN + used))
            for j, used in enumerate((-1, 0, 2, 4)):
                n = NSLOT - 4 + j
                split(j, n, 16 * (n // RAW) + 16, E_FFN + PER_FB * (NFB - 1) + used)
            for c in range(CHUNKS):
                cs = slice(c * CH, (c + 1) * CH)
                pool.wait_ge(y_sc, c + 1)
                pool.tensor_tensor(ma[:, 4:8, cs], mix[:, 4:8, cs], ma[:, 4:8, cs], ALU.add
                                   ).then_inc(y_pool, 1)

        @block.tensor
        def _(pe):
            PARTS = ((0, 0), (0, 1), (1, 0))
            W = (w_h, w_l)
            XN = (xn_h, xn_l)
            pe.sem_inc(mm, HL)
            pe.sem_inc(ret_b, 1)

            def tile_mms(place_, sub, xs, k, g, first, last, chunks=range(CHUNKS)):
                for n, (a, b) in enumerate(PARTS):
                    for c in chunks:
                        out = pe.matmul(pch(g, c), W[a][:, place_, sub * P:(sub + 1) * P],
                                        xs[b][:, k, c * CH:(c + 1) * CH],
                                        start=(first and n == 0), stop=(last and n == 2))
                return out

            def group8(g, slot, xs, gshift=0, sshift=0):
                free_set(pe, g, gshift)
                for half in range(2):
                    pe.wait_ge(w_split, sshift + (slot + half + 1))
                    for sub in range(SLOT_TILES):
                        k = SLOT_TILES * half + sub
                        out = tile_mms((slot + half) % HL, sub, xs, k, g, k == 0, k == KT - 1)
                    out.then_inc(mm, 1)

            def stat_group(g, src, n, sem_):
                free_set(pe, g)
                for c in range(CHUNKS):
                    for j in range(n):
                        out = pe.matmul(pch(g, c), ones[:], src(j, c), start=(j == 0), stop=(j == n - 1))
                out.then_inc(sem_, 1)

            pe.wait_ge(c_init, 1)
            for c in range(CHUNKS):
                pe.wait_ge(x_sq, c + 1)
                for k in range(KT):
                    out = pe.matmul(pch(G_XSTAT, c), ones[:], xsq[:, c, k * CH:(k + 1) * CH],
                                    start=(k == 0), stop=(k == KT - 1))
                out.then_inc(x_st, 1)

            pe.wait_ge(w_split, 2)
            for c in range(CHUNKS):
                pe.wait_ge(xn_hi, c + 1)
                pe.wait_ge(xn_lo, c + 1)
                for k in range(KT):
                    out = tile_mms(k // SLOT_TILES, k % SLOT_TILES, XN, k, G_U, k == 0, k == KT - 1, (c,))
                    if c == CHUNKS - 1 and k == SLOT_TILES - 1:
                        out.then_inc(mm, 1)
            out.then_inc(mm, 1)
            group8(G_U + 1, S_U + 2, XN)
            with pe.Fori(0, CT - 1) as i:
                group8(G_U + 2, S_U + 4, XN, i, i * 4)
                group8(G_U + 3, S_U + 6, XN, i, i * 4)

            def qkv(p):
                with pe.Fori(0, 4) as i:
                    group8(G_QKV[p], S_QKV[p], XN, i, i * 4)
                    group8(G_QKV[p] + 1, S_QKV[p] + 2, XN, i, i * 4)

            def v_decode(p):
                if p:
                    pe.wait_ge(s_upd, (1 + NRC) * p)
                for t in range(4):
                    out = pe.transpose(ps[0:DEC, 7, t * P:(t + 1) * P], vv[p][:, t, SEQ:T], ident[:])
                out.then_inc(vs_T, 1)

            def chunk_a(p, n, col):
                pe.wait_ge(staged, n * 2 + 2)
                pe.wait_ge(o_out, n + 1)
                pe.wait_ge(s_upd, n + (p + 1))
                for h in range(2):
                    pe.matmul(B6[:, h * RC:(h + 1) * RC], kt_b[:, h, :], qk[p][:, h, bass.ds(col, RC)],
                              start=True, stop=True)
                for h in range(2):
                    pe.transpose(B6[:, (2 + h) * RC:(3 + h) * RC], kt_b[:, h, :], ident[:])
                for t in range(4):
                    out = pe.transpose(B7[:, t * RC:(t + 1) * RC], vt_b[:, t, :], ident[:])
                out.then_inc(ret_a, 1)

            def chunk_b(p, n, col):
                pe.wait_ge(vt_rdy, n + 1)
                pe.wait_ge(pk_rdy, n * 3 + 3)
                for h in range(2):
                    for e in range(2):
                        o = B6[:, (2 * h + e) * RC:(2 * h + e + 1) * RC]
                        pe.matmul(o, vt_b[:, 2 * h + e, :], p_b[:, h, :], start=True, stop=False)
                        pe.matmul(o, state[:, h, e * P:(e + 1) * P], qk[p][:, h, bass.ds(col, RC)],
                                  start=False, stop=True)
                for h in range(2):
                    out = pe.matmul(B7[:, h * DV:(h + 1) * DV], kt_b[:, h, :],
                                    vt_b[:, 2 * h:2 * h + 2, :].rearrange("p a n -> p (a n)"),
                                    start=True, stop=True)
                out.then_inc(ret_b, 1)

            def decode_out(p, g, j, u, n, b):
                pe.wait_ge(s_new, n + 2)
                for h in range(2):
                    for e in range(2):
                        at_ = CH + 8 + 4 * j + 2 * h + e
                        out = pe.matmul(ps[:, 3 * (g % 2), at_:at_ + 1],
                                        s_dec[:, u % 2, h * DV + e * P:h * DV + (e + 1) * P],
                                        qk[p][:, h, bass.ds(b, 1)], start=True, stop=True)
                return out

            def ret_slot(p, g, slot, xs, k0, ktiles, u, c, gshift, sshift):
                n = c + NRC * p
                if k0 == 0:
                    free_set(pe, g, gshift)
                pe.wait_ge(w_split, sshift + (slot + 1))
                for half in range(2):
                    for sub in (2 * half, 2 * half + 1):
                        k = k0 + sub
                        out = tile_mms(slot % HL, sub, xs, k, g, k == 0, k == ktiles - 1)
                    if half == 0:
                        chunk_a(p, n, c * RC)
                    else:
                        last = out
                return last, n

            qkv(0)
            with pe.Fori(0, 2) as i:
                group8(G_G[0], S_G[0], XN, i, i * 4)
                group8(G_G[0] + 1, S_G[0] + 2, XN, i, i * 4)

            group8(G_GA, S_GA, XN)
            group8(G_GA + 1, S_GA + 2, XN)
            pe.wait_ge(cv_acc, 2 * TAPS * CT)
            pe.wait_ge(h_done, 2 * CT)
            stat_group(G_LNM, lambda j, c: conv[:, j, c * CH:(c + 1) * CH], CT, lnm_st)
            v_decode(0)
            group8(G_LNM + 1, S_GA + 4, XN)
            group8(G_LNM + 2, S_GA + 6, XN)
            pe.wait_ge(ln_sq, CT)
            stat_group(G_LNV, lambda j, c: u_ext[:, j, c * CH:(c + 1) * CH], CT, lnv_st)
            with pe.Fori(0, 2) as i:
                group8(G_LNV + 1, S_GA + 8, XN, i, i * 4)
                group8(G_LNV + 2, S_GA + 10, XN, i, i * 4)

            pe.wait_ge(cv_hi, CT)
            pe.wait_ge(cv_lo, CT)
            pe.wait_ge(rope_done, 2 * CHUNKS)
            with pe.Fori(0, NRC // 2) as i:
                for u in range(2):
                    g = G_AOUT + u
                    c = i * 2 + u
                    out, n = ret_slot(0, g, S_AOUT + u, (cv_h, cv_l), 0, CT, u, c, i, i * 2)
                    chunk_b(0, n, c * RC)
                    decode_out(0, g, 0, u, n, c + SEQ).then_inc(mm, 1)

            def out_stats(p):
                for h in range(2):
                    g = G_ON[p] + h
                    free_set(pe, g)
                    for c in range(CHUNKS):
                        pe.wait_ge(on_sq, 6 * p + 3 * h + c + 1)
                        for e in range(2):
                            out = pe.matmul(pch(g, c), ones[:], osq[:, (3 * h + c) % 2, e * CH:(e + 1) * CH],
                                            start=(e == 0), stop=(e == 1))
                        out.then_inc(on_st, 1)

            out_stats(0)
            qkv(1)
            pe.wait_ge(rope_done, 4 * CHUNKS)
            taken(pe, G_QKV[1] + 7)
            v_decode(1)
            with pe.Fori(0, 2) as i:
                for t in range(2):
                    g = G_G[1] + t
                    for half in range(2):
                        u = 2 * t + half
                        c = i * 4 + u
                        out, n = ret_slot(1, g, S_G[1] + u, XN, 4 * half, KT, u, c, i, i * 4)
                        if half == 0:
                            out.then_inc(mm, 1)
                        chunk_b(1, n, c * RC)
                    for j in range(2):
                        last = decode_out(1, g, j, j, n - 1 + j, c - 1 + j + SEQ)
                    last.then_inc(mm, 1)
            out_stats(1)

            with pe.Fori(0, KT) as i:
                group8(G_GB, S_GB, XN, i, i * 4)
                g, slot = G_GB + 1, S_GB + 2
                free_set(pe, g, i)
                pe.wait_ge(ro_hi, 8)
                pe.wait_ge(ro_lo, 8)
                for half in range(2):
                    pe.wait_ge(w_split, i * 4 + (slot + half + 1))
                    for sub in range(SLOT_TILES):
                        out = tile_mms((slot + half) % HL, sub, (ro_h[half], ro_l[half]), sub, g,
                                       half == 0 and sub == 0, half == 1 and sub == 3)
                    out.then_inc(mm, 1)

            pe.wait_ge(mg_hi, KT)
            pe.wait_ge(mg_lo, KT)
            with pe.Fori(0, KT // 2) as i:
                group8(G_WO, S_WO, (mg_h, mg_l), i, i * 4)
                group8(G_WO + 1, S_WO + 2, (mg_h, mg_l), i, i * 4)
            pe.wait_ge(wo_sum, KT + 2)
            free_set(pe, G_MSTAT)
            for c in range(CHUNKS):
                pe.matmul(pch(G_MSTAT, c), ones[:], gbuf[:, 3, c * CH:(c + 1) * CH],
                          start=True, stop=True).then_inc(m_st, 1)

            FX = (fx_h, fx_l)
            HID = (hid_h, hid_l)
            free_set(pe, G_FFN)
            pe.wait_ge(w_split, S_FFN + 2)
            for c in range(CHUNKS):
                pe.wait_ge(fx_hi, c + 1)
                pe.wait_ge(fx_lo, c + 1)
                for k in range(KT):
                    out = tile_mms(k // SLOT_TILES, k % SLOT_TILES, FX, k, G_FFN, k == 0, k == KT - 1, (c,))
                    if c == CHUNKS - 1 and k == SLOT_TILES - 1:
                        out.then_inc(mm, 1)
            out.then_inc(mm, 1)
            group8(G_FFN + 1, S_FFN + 2, FX)

            def down(b, g, slot, gshift, sshift, hshift):
                pe.wait_ge(hid_hi, hshift + 2 * (b + 1))
                pe.wait_ge(hid_lo, hshift + (2 * (b + 1) + 2))
                for m in range(KT):
                    free_set(pe, g + m, gshift)
                    if m % 2 == 0:
                        pe.wait_ge(w_split, sshift + (slot + m // 2 + 1))
                    for k in range(FB):
                        out = tile_mms((slot + m // 2) % HL, FB * (m % 2) + k, HID, FB * (b % 2) + k,
                                       g + m, k == 0, k == FB - 1)
                    out.then_inc(mm, 1)

            def up_down(b, gshift=0, sshift=0, hshift=0):
                g, slot = G_FFN + 2 + 10 * b, S_FFN + 4 + 8 * b
                group8(g, slot, FX, gshift, sshift)
                group8(g + 1, slot + 2, FX, gshift, sshift)
                down(b, g + 2, slot + 4, gshift, sshift, hshift)

            with pe.Fori(0, (NFB - 2) // 2) as i:
                up_down(0, i * 10, i * 16, i * 4)
                up_down(1, i * 10, i * 16, i * 4)
            up_down(NFB - 2)
            pe.wait_ge(h_sum, KT + 1)
            for c in range(CHUNKS):
                if c == 2:
                    pe.wait_ge(h_ms, 1)
                pe.matmul(ps[:, 6 + c % 2, 0:CH], ones[:], hsum[:, c * CH:(c + 1) * CH],
                          start=True, stop=True).then_inc(h_st, 1)
            down(NFB - 1, G_FSTAT - 8, NSLOT - 4, 0, 0, 0)
            pe.wait_ge(f_sum, KT + 1)
            free_set(pe, G_FSTAT)
            for c in range(CHUNKS):
                pe.matmul(pch(G_FSTAT, c), ones[:], gbuf[:, 3, c * CH:(c + 1) * CH],
                          start=True, stop=True).then_inc(f_st, 1)

        @block.scalar
        def _(act):
            def rsqrt_mean(src, n, ln_sem, rs_sem, count):
                act.activation(src, src, ACT.Ln, bias=eps_b[:], scale=1.0 / n).then_inc(ln_sem, 1)
                act.wait_ge(ln_sem, count)
                return act.activation(src, src, ACT.Exp, scale=-0.5).then_inc(rs_sem, 1)

            act.dma_start(vec[:], vecs).then_inc(cst_ld, 16)
            act.dma_start(ident[:], ident_d).then_inc(cst_ld, 16)
            act.dma_start(mask[:], mask_d).then_inc(cst_ld, 16)
            act.dma_start(wdw[:], wdwT).then_inc(wdw_ld, 16)
            act.dma_start(hist[:], cacheT).then_inc(hist_ld, 16)
            act.sem_inc(o_out, 1)
            act.sem_inc(ss_st[0], 16)
            act.sem_inc(ss_st[1], 16)

            def x_square(c):
                act.wait_ge(x_ld[c], 16)
                act.activation(xsq[:, c, :].rearrange("p (k n) -> p k n", k=KT),
                               x_in[:, :, c * CH:(c + 1) * CH], ACT.Square).then_inc(x_sq, 1)

            def x_rms(c):
                act.wait_ge(x_st, c + 1)
                rsqrt_mean(pch(G_XSTAT, c), D_MODEL, x_ln, x_rs, c + 1)

            def x_hi(c):
                if c == 0:
                    act.wait_ge(cst_ld, 48)
                if c < CHUNKS - 1:
                    act.wait_ge(x_sc, c + 1)
                else:
                    taken(act, G_XSTAT)
                for k in range(KT):
                    out = act.activation(xn_h[:, k, c * CH:(c + 1) * CH], x_in[:, k, c * CH:(c + 1) * CH],
                                         ACT.Copy, scale=vec[:, V_PRE + k:V_PRE + k + 1])
                out.then_inc(xn_hi, 1)

            x_square(0)
            act.wait_ge(c_init, 3)
            x_rms(0)
            x_square(1)
            x_hi(0)
            x_rms(1)
            x_square(2)
            x_hi(1)
            x_rms(2)
            x_hi(2)

            act.wait_ge(x_st, CHUNKS)
            act.dma_start(rope0[:], rope[0]).then_inc(tab_ld[0], 16)

            for j in range(CT):
                g = G_U + 2 * j
                act.wait_ge(mm, done(S_U + 4 * j + 1))
                if j:
                    taken(act, g - 1)
                act.activation(t3(sgt[:]), pset(g), ACT.Sigmoid).then_inc(ps_free[g % 2], 1)

            def qkv_out(p):
                for t in range(8):
                    g = G_QKV[p] + t
                    act.wait_ge(mm, done(S_QKV[p] + 2 * t + 1))
                    if t == 0 and p == 0:
                        act.wait_ge(xn_lo, CHUNKS)
                    if t >= 4:
                        act.wait_ge(rope_done, 2 * CHUNKS * p + CHUNKS * (1 + (t - 4) // 2))
                    act.activation(t3(vv[p][:, t % 4, :]), pset(g), ACT.Copy).then_inc(ps_free[g % 2], 1)

            qkv_out(0)
            act.wait_ge(h_done, 2 * CT)
            act.dma_start(convp, u_ext[:, :, SEQ:SEQ + HIST]).then_inc(cv_out, 16)
            act.dma_start(convs, hist[:]).then_inc(cv_out, 16)
            act.wait_ge(cv_out, 32)
            for t in range(4):
                g = G_G[0] + t
                act.wait_ge(mm, done(S_G[0] + 2 * t + 1))
                act.activation(t3(gbuf[:, t, :]), pset(g), ACT.Sigmoid).then_inc(g_sg, 1)

            def ga_out(m):
                g = G_GA + m + (m >= 2) + (m >= 4)
                act.wait_ge(mm, done(S_GA + 2 * m + 1))
                act.activation(t3(ma[:, m, :]), pset(g), ACT.Sigmoid).then_inc(ps_free[g % 2], 1)

            act.wait_ge(rope_done, 2 * CHUNKS)
            ga_out(0)
            ga_out(1)
            for j in range(CT):
                if j < CT - 1:
                    act.wait_ge(ln_xc, j + 1)
                else:
                    taken(act, G_LNM)
                act.activation(u_ext[:, j, 0:T], conv[:, j, :], ACT.Square).then_inc(ln_sq, 1)

            def v_decode_out(p):
                act.wait_ge(vs_T, p + 1)
                act.activation(vt_b[0:DEC].rearrange("p a n -> p (a n)"), ps[0:DEC, 7, :],
                               ACT.Copy).then_inc(vs_cp, 1)
                act.wait_ge(vs_cp, p + 1)
                act.dma_start(vscr[p], vt_b[0:DEC].rearrange("p a n -> p (a n)")).then_inc(vs_st, 16)

            v_decode_out(0)
            ga_out(2)
            ga_out(3)
            act.wait_ge(lnv_st, 1)
            rsqrt_mean(pset(G_LNV), CONV_DIM, ln_ln, ln_rs, 1)
            for j in range(CT):
                if j < CT - 1:
                    act.wait_ge(ln_n, j + 1)
                else:
                    taken(act, G_LNV)
                act.activation(u_ext[:, j, 0:T], conv[:, j, :], ACT.Sigmoid,
                               bias=vec[:, V_LNB + j:V_LNB + j + 1],
                               scale=vec[:, V_LNW + j:V_LNW + j + 1]).then_inc(ln_sg, 1)
            ga_out(4)
            for j in range(CT):
                act.wait_ge(ln_y, j + 1)
                act.activation(cv_h[:, j, 0:T], conv[:, j, :], ACT.Copy).then_inc(cv_hi, 1)
                if j:
                    ga_out(4 + j)

            def chunk_io(p, n, b, u, pe_done):
                w = u % 2
                act.wait_ge(ss_st[w], (n // 2) * 16 + 16 if isinstance(n, int) else pe_done[1])
                act.wait_ge(mm, pe_done[0])
                act.dma_start(s_dec[:, w, :].rearrange("p (h e) -> p h e", h=2),
                              s_in[bass.ds(b, 1), 2 * p:2 * p + 2].rearrange("a h p e -> p (a h) e")
                              ).then_inc(ss_ld[w], 16)
                act.wait_ge(s_new, n + 1)
                act.dma_start(v_bc[:], vscr[p, bass.ds(b, 1), :].broadcast_to([P, 2 * DV])
                              ).then_inc(vb_ld, 16)
                act.wait_ge(ret_b, n + 1)
                act.sem_inc(turns, 1)
                act.activation(kt_b[:], qk[p][:, 2:4, bass.ds(b * RC, RC)], ACT.Copy).then_inc(staged, 1)
                act.activation(vt_b[:], vv[p][:, :, bass.ds(b * RC, RC)], ACT.Copy).then_inc(staged, 1)

            def chunk_out(p, n, b, u):
                act.wait_ge(ret_a, n + 1)
                act.activation(vt_b[:], B7.rearrange("p (a n) -> p a n", a=4), ACT.Copy).then_inc(vt_rdy, 1)
                act.wait_ge(ret_b, n + 2)
                act.sem_inc(turns, 1)
                act.activation(vv[p][:, :, bass.ds(b * RC, RC)], B6.rearrange("p (a n) -> p a n", a=4),
                               ACT.Copy).then_inc(o_out, 1)
                act.wait_ge(s_new, n + 2)
                act.dma_start(rets[bass.ds(b, 1), 2 * p:2 * p + 2].rearrange("a h p e -> p (a h) e"),
                              s_dec[:, u % 2, :].rearrange("p (h e) -> p h e", h=2)
                              ).then_inc(ss_st[u % 2], 16)

            def ret_tail(p, last_group):
                act.wait_ge(s_upd, (1 + NRC) * (p + 1))
                act.dma_start(retp[2 * p:2 * p + 2].rearrange("h p e -> p h e"),
                              state[:]).then_inc(rp_st, 16)
                taken(act, last_group)
                for w in range(2):
                    act.wait_ge(ss_st[w], 16 + 16 * (DEC // 2) * (p + 1))
                for h in range(2):
                    for c in range(CHUNKS):
                        i = 6 * p + 3 * h + c
                        if i >= 2:
                            act.wait_ge(on_st, i - 1)
                        act.activation(osq[:, i % 2, :].rearrange("p (a n) -> p a n", a=2),
                                       vv[p][:, 2 * h:2 * h + 2, c * CH:(c + 1) * CH],
                                       ACT.Square).then_inc(on_sq, 1)
                    act.wait_ge(on_st, 6 * p + 3 * h + 3)
                    rsqrt_mean(pset(G_ON[p] + h), DV, on_ln, on_rs, 2 * p + h + 1)
                for t in range(4):
                    act.wait_ge(ro_g, 4 * p + t + 1)
                    act.activation(ro_h[p][:, t, :], vv[p][:, t, :], ACT.Copy).then_inc(ro_hi, 1)

            act.wait_ge(rope_done, 2 * CHUNKS)
            act.wait_ge(vs_st, 16)
            with act.Fori(0, NRC // 2) as i:
                for u in range(2):
                    c = i * 2 + u
                    chunk_io(0, c, c, u, (i * 2 + (done(S_AOUT) + u - 2), i * 16 + 16))
                    chunk_out(0, c, c, u)
            ret_tail(0, G_AOUT + 7)

            act.wait_ge(ro_g, 4)
            act.dma_start(rope1[:], rope[1]).then_inc(tab_ld[1], 16)
            qkv_out(1)
            v_decode_out(1)
            act.wait_ge(rope_done, 4 * CHUNKS)
            act.wait_ge(vs_st, 32)
            with act.Fori(0, NRC // 4) as i:
                for u in range(4):
                    c = i * 4 + u
                    n = c + NRC
                    chunk_io(1, n, c, u, (i * 4 + (done(S_G[1]) - 1 + 2 * (u // 2)),
                                          i * 32 + (16 * (u // 2) + 16 + 16 * (DEC // 2))))
                    chunk_out(1, n, c, u)
                    if u % 2:
                        t = u // 2
                        act.wait_ge(mm, i * 4 + done(S_G[1] + 2 * t + 1))
                        act.sem_inc(turns, 1)
                        act.activation(t3(gbuf[:, bass.ds(i * 2 + t, 1), :].rearrange("p a n -> p (a n)")),
                                       pset(G_G[1] + t), ACT.Sigmoid).then_inc(g_sg, 1)
            ret_tail(1, G_G[1] + 3)

            def gb_out(gs, ss):
                act.wait_ge(mm, ss + done(S_GB + 1))
                taken(act, G_GB - 1, gs)
                act.activation(t3(gbuf[:, 0, :]), pset(G_GB), ACT.Sigmoid).then_inc(ps_free[G_GB % 2], 1)

            act.wait_ge(ro_lo, 8)
            with act.Fori(0, KT - 1) as i:
                gb_out(i, i * 4)
            gb_out(KT - 1, 4 * (KT - 1))
            for m in range(KT):
                act.wait_ge(mg_rdy, m + 2)
                act.activation(mg_h[:, m, :], ma[:, m, :], ACT.Copy).then_inc(mg_hi, 1)
            act.wait_ge(mm, done(S_WO - 1))
            act.dma_start(x_again[:], xT).then_inc(xa_ld, 16)

            with act.Fori(0, KT // 2) as i:
                for u in range(2):
                    g = G_WO + u
                    act.wait_ge(mm, i * 4 + done(S_WO + 2 * u + 1))
                    act.wait_ge(wo_sum, i * 2 + (u + 1))
                    act.activation(t3(gbuf[:, 1 + u, :]), pset(g), ACT.Square).then_inc(wo_sq, 1)
                    act.activation(t3(mix[:, bass.ds(i * 2 + u, 1), :].rearrange("p a n -> p (a n)")),
                                   pset(g), ACT.Copy,
                                   scale=vec[:, bass.ds(i * 2 + (V_POST + u), 1)]).then_inc(ps_free[g % 2], 1)

            def m_rms(c):
                act.wait_ge(m_st, c + 1)
                rsqrt_mean(pch(G_MSTAT, c), D_MODEL, m_ln, m_rs, c + 1)

            for c in range(CHUNKS):
                m_rms(c)
            for c in range(CHUNKS):
                act.wait_ge(h_pool, c + 1)
                if c < CHUNKS - 1:
                    act.wait_ge(h_dve, c + 1)
                else:
                    taken(act, G_MSTAT)
                for k in range(KT):
                    out = act.activation(fx_h[:, k, c * CH:(c + 1) * CH], ma[:, k, c * CH:(c + 1) * CH],
                                         ACT.Copy, scale=vec[:, V_FPRE + k:V_FPRE + k + 1])
                out.then_inc(fx_hi, 1)

            def up_out(g, b, j, ev, n, gshift=0):
                act.wait_ge(mm, ev)
                act.activation(t3(gbuf[:, j, :]), pset(g), ACT.Relu).then_inc(ps_free[g % 2], 1)
                taken(act, g, gshift)
                act.wait_ge(hid_lo, n + 1)
                act.activation(gbuf[:, 2 + j, :], gbuf[:, j, :], ACT.Square).then_inc(hid_t, 1)
                act.activation(hid_h[:, FB * (b % 2) + j, :], gbuf[:, j, :], ACT.Square).then_inc(hid_hi, 1)

            for j in range(FB):
                up_out(G_FFN + j, 0, j, done(S_FFN + 2 * j + 1), j)
            with act.Fori(0, (NFB - 2) // 2) as i:
                for v in range(2):
                    for j in range(FB):
                        up_out(G_FFN + 2 + 10 * v + j, v + 1, j, i * (2 * PER_FB) + (E_FFN + PER_FB * v + 2 * (j + 1)),
                               i * 4 + (2 * (v + 1) + j), i * 10)
            b = NFB - 1
            for j in range(FB):
                up_out(G_FFN + 2 + 10 * (b - 1) + j, b, j, E_FFN + PER_FB * (b - 1) + 2 * (j + 1), 2 * b + j)

            for k in range(KT):
                act.wait_ge(h_sum, k + 1)
                act.activation(hsq[:], ma[:, k, :], ACT.Square).then_inc(h_sq, 1)
            for c in range(CHUNKS):
                act.wait_ge(h_st, c + 1)
                if c == 0:
                    act.wait_ge(h_st, CHUNKS - 1)
                act.activation(hms[:, c * CH:(c + 1) * CH], ps[:, 6 + c % 2, 0:CH], ACT.Square,
                               bias=eps15_b[:], scale=EPS ** 0.5 / D_MODEL).then_inc(h_ms, 1)
            for m in range(KT):
                taken(act, G_FSTAT - 8 + m)
                if m >= 2:
                    act.wait_ge(f_sum, m)
                act.activation(gbuf[:, m % 2, :], mix[:, m, :], ACT.Square).then_inc(f_sq, 1)
            for c in range(CHUNKS):
                act.wait_ge(f_den, c + 1)
                act.activation(pch(G_FSTAT, c), pch(G_FSTAT, c), ACT.Ln).then_inc(f_ln, 1)
                act.wait_ge(f_ln, c + 1)
                act.activation(pch(G_FSTAT, c), pch(G_FSTAT, c), ACT.Exp, scale=-0.5).then_inc(f_rs, 1)

        @block.vector
        def _(dve):
            steps = [0]

            def step(instruction):
                instruction.then_inc(dve_c, 1)
                steps[0] += 1
                dve.wait_ge(dve_c, steps[0])

            dve.memset(ones[:], 1.0).then_inc(c_init, 1)
            dve.memset(eps_b[:], EPS).then_inc(c_init, 1)
            dve.memset(eps15_b[:], EPS ** 1.5).then_inc(c_init, 1)
            dve.sem_inc(s_new, 1)
            dve.sem_inc(wo_sum, 1)
            dve.sem_inc(hid_lo, 2)
            dve.sem_inc(mg_rdy, 1)
            step(dve.memset(u_ext[:, :, 0:HIST], 0.0))

            for c in range(CHUNKS):
                cs = slice(c * CH, (c + 1) * CH)
                dve.wait_ge(x_rs, c + 1)
                dve.tensor_tensor(x_in[:, :, cs], x_in[:, :, cs],
                                  pch(G_XSTAT, c).unsqueeze(1).broadcast_to([P, KT, CH]), ALU.mult
                                  ).then_inc(x_sc if c < CHUNKS - 1 else ps_free[G_XSTAT % 2], 1)
                dve.wait_ge(xn_hi, c + 1)
                for k in range(KT):
                    out = dve.scalar_tensor_tensor(xn_l[:, k, cs], x_in[:, k, cs], vec[:, V_PRE + k:V_PRE + k + 1],
                                                   xn_h[:, k, cs].bitcast(F32), ALU.mult, ALU.subtract)
                out.then_inc(xn_lo, 1)

            HALF = SEQ // 2
            cursor = [0]

            def tap(j, k, shift=0, i=None):
                for half in range(2):
                    bank = ps[:, 6 + half, :]
                    idx = k if i is None else i
                    u_ = (u_ext[:, j, k + HALF * half:k + HALF * (half + 1)] if i is None
                          else u_ext[:, j, bass.ds(i + HALF * half, HALF)])
                    w_ = wdw[:, j, k:k + 1] if i is None else wdw[:, j, bass.ds(i, 1)]
                    n = 2 * TAPS * j + half - 1
                    if i is not None or n + 2 * k > 0:
                        dve.wait_ge(cv_acc, (2 * k + n) if i is None else i * 2 + n)
                    if i is None and k == 0:
                        out = dve.tensor_scalar(bank, u_, w_, vec[:, V_BDW + j:V_BDW + j + 1], ALU.mult, ALU.add)
                    else:
                        dst = conv[:, j, HALF * half:HALF * (half + 1)] if (i is None and k == TAPS - 1) else bank
                        out = dve.scalar_tensor_tensor(dst, u_, w_, bank, ALU.mult, ALU.add)
                    out.then_inc(cv_acc, 1)

            def taps(n):
                while n > 0 and cursor[0] < TAPS * CT:
                    j, k = divmod(cursor[0], TAPS)
                    if k in (0, TAPS - 1):
                        tap(j, k)
                        took = 1
                    else:
                        took = min(n, TAPS - 1 - k)
                        with dve.Fori(k, k + took) as i:
                            tap(j, None, i=i)
                    cursor[0] += took
                    n -= took

            dve.wait_ge(wdw_ld, 16)
            dve.wait_ge(hist_ld, 16)
            for j in range(CT):
                g = G_U + 1 + 2 * j
                dve.wait_ge(mm, done(S_U + 4 * j + 3))
                taken(dve, g - 1)
                dve.tensor_tensor(t3(u_ext[:, j, HIST:HIST + T]), pset(g), t3(sgt[:]), ALU.mult
                                  ).then_inc(ps_free[g % 2], 1)
                taken(dve, g)
                dve.tensor_copy(hist[:, j, :, HIST], u_ext[:, j, HIST + SEQ:HIST + T]).then_inc(h_done, 1)
                dve.wait_ge(h_done, 2 * j + 1)
                step(dve.tensor_tensor(hprod[:], hist[:, j], wdw[:, j, :].unsqueeze(1).broadcast_to([P, DEC, TAPS]),
                                       ALU.mult))
                step(dve.reduce_sum(conv[:, j, SEQ:T], hprod[:], mybir.AxisListType.X))
                dve.tensor_scalar(conv[:, j, SEQ:T], conv[:, j, SEQ:T], vec[:, V_BDW + j:V_BDW + j + 1], None,
                                  ALU.add).then_inc(h_done, 1)
                taps((14, 14, 14, 13)[j])

            def rotate(p, w):
                taken(dve, G_QKV[p] + 2 * w)
                taken(dve, G_QKV[p] + 2 * w + 1)
                for c in range(CHUNKS):
                    cs = slice(c * CH, (c + 1) * CH)
                    first, second = vv[p][:, 2 * w, cs], vv[p][:, 2 * w + 1, cs]
                    if 2 * p + w + c > 0:
                        dve.wait_ge(rope_done, CHUNKS * (2 * p + w) + c)
                    cos, sin = rtab[p][:, 2 * w, cs], rtab[p][:, 2 * w + 1, cs]
                    for k, (a, b) in enumerate(((first, cos), (second, sin), (second, cos), (first, sin))):
                        out = dve.tensor_tensor(rtmp[p][:, k, :], a, b, ALU.mult)
                    out.then_inc(rope_p, 1)
                    dve.wait_ge(rope_p, 2 * CHUNKS * p + CHUNKS * w + c + 1)
                    for h in range(2):
                        hs = slice(64 * h, 64 * h + 64)
                        dve.tensor_tensor(qk[p][0:64, 2 * w + h, cs], rtmp[p][hs, 0, :], rtmp[p][hs, 1, :],
                                          ALU.subtract)
                        out = dve.tensor_tensor(qk[p][64:128, 2 * w + h, cs], rtmp[p][hs, 2, :], rtmp[p][hs, 3, :],
                                                ALU.add)
                    out.then_inc(rope_done, 1)

            dve.wait_ge(tab_ld[0], 16)
            dve.wait_ge(xn_hi, CHUNKS)
            rotate(0, 0)
            taps(3)
            rotate(0, 1)
            taps(17)
            for t in range(4):
                g = G_G[0] + t
                dve.wait_ge(g_sg, t + 1)
                dve.tensor_tensor(t3(gbuf[:, t, :]), pset(g), t3(gbuf[:, t, :]), ALU.mult
                                  ).then_inc(ps_free[g % 2], 1)
                taps(7 if t < 3 else TAPS * CT)

            dve.wait_ge(lnm_st, 1)
            for j in range(CT):
                dve.scalar_tensor_tensor(t3(conv[:, j, :]), pset(G_LNM), -1.0 / CONV_DIM, t3(conv[:, j, :]),
                                         ALU.mult, ALU.add
                                         ).then_inc(ln_xc if j < CT - 1 else ps_free[G_LNM % 2], 1)
            dve.wait_ge(ln_rs, 1)
            for j in range(CT):
                dve.tensor_tensor(t3(conv[:, j, :]), t3(conv[:, j, :]), pset(G_LNV), ALU.mult
                                  ).then_inc(ln_n if j < CT - 1 else ps_free[G_LNV % 2], 1)
            for j in range(CT):
                dve.wait_ge(ln_sg, j + 1)
                dve.tensor_scalar(conv[:, j, :], conv[:, j, :], vec[:, V_LNW + j:V_LNW + j + 1],
                                  vec[:, V_LNB + j:V_LNB + j + 1], ALU.mult, ALU.add).then_inc(ln_z, 1)
                dve.wait_ge(ln_z, j + 1)
                dve.tensor_tensor(conv[:, j, :], conv[:, j, :], u_ext[:, j, 0:T], ALU.mult).then_inc(ln_y, 1)
            for j in range(CT):
                dve.wait_ge(cv_hi, j + 1)
                dve.tensor_tensor(cv_l[:, j, :], conv[:, j, :], cv_h[:, j, 0:T].bitcast(F32), ALU.subtract
                                  ).then_inc(cv_lo, 1)

            def chunk(p, n, b, u, loads):
                dve.wait_ge(ret_a, n + 1)
                dve.tensor_tensor(p_b[:], B6[:, 0:2 * RC].rearrange("p (h n) -> p h n", h=2),
                                  mask[:].unsqueeze(1).broadcast_to([P, 2, RC]), ALU.mult).then_inc(pk_rdy, 1)
                for h in range(2):
                    dve.tensor_scalar(kt_b[:, h, :], B6[:, (2 + h) * RC:(3 + h) * RC],
                                      float(GAMMA[2 * p + h] ** RC), None, ALU.mult).then_inc(pk_rdy, 1)
                dve.wait_ge(ss_ld[u % 2], loads)
                dve.wait_ge(vb_ld, n * 16 + 16)
                for h in range(2):
                    hs = slice(h * DV, (h + 1) * DV)
                    dve.tensor_scalar(v_bc[:, hs], v_bc[:, hs], qk[p][:, 2 + h, bass.ds(b + SEQ, 1)], None,
                                      ALU.mult).then_inc(s_kv, 1)
                dve.wait_ge(s_kv, n * 2 + 2)
                for h in range(2):
                    hs = slice(h * DV, (h + 1) * DV)
                    out = dve.scalar_tensor_tensor(s_dec[:, u % 2, hs], s_dec[:, u % 2, hs], float(GAMMA[2 * p + h]),
                                                   v_bc[:, hs], ALU.mult, ALU.add)
                out.then_inc(s_new, 1)
                dve.wait_ge(ret_b, n + 2)
                dve.wait_ge(s_upd, n + (p + 1))
                for h in range(2):
                    out = dve.scalar_tensor_tensor(state[:, h, :], state[:, h, :], float(GAMMA[2 * p + h] ** RC),
                                                   B7[:, h * DV:(h + 1) * DV], ALU.mult, ALU.add)
                out.then_inc(s_upd, 1)

            def normed_outputs(p):
                for h in range(2):
                    g = G_ON[p] + h
                    dve.wait_ge(on_rs, 2 * p + h + 1)
                    for t in (2 * h, 2 * h + 1):
                        dve.tensor_tensor(t3(vv[p][:, t, :]), t3(vv[p][:, t, :]), pset(g), ALU.mult
                                          ).then_inc(on_n if t % 2 == 0 else ps_free[g % 2], 1)
                    taken(dve, g)
                    for t in (2 * h, 2 * h + 1):
                        dve.tensor_tensor(vv[p][:, t, :], vv[p][:, t, :], gbuf[:, t, :], ALU.mult).then_inc(ro_g, 1)
                for t in range(4):
                    dve.wait_ge(ro_hi, 4 * p + t + 1)
                    dve.tensor_tensor(ro_l[p][:, t, :], vv[p][:, t, :], ro_h[p][:, t, :].bitcast(F32), ALU.subtract
                                      ).then_inc(ro_lo, 1)

            dve.memset(state[:], 0.0).then_inc(s_upd, 1)
            dve.wait_ge(cst_ld, 48)
            taken(dve, G_LNV + 3)
            taken(dve, G_LNV + 4)
            with dve.Fori(0, NRC // 2) as i:
                for u in range(2):
                    c = i * 2 + u
                    g = G_AOUT + u
                    chunk(0, c, c, u, i * 16 + 16)
                    dve.wait_ge(mm, i * 2 + done(S_AOUT + u))
                    dve.tensor_copy(v0[:, :, bass.ds(c + SEQ, 1)].rearrange("p t a -> p (t a)"),
                                    ps[:, 3 * (g % 2), CH + 8:CH + 12])
                    tile_ = t3(ma[:, bass.ds(c, 1), :].rearrange("p a n -> p (a n)"))
                    dve.tensor_tensor(tile_, pset(g), tile_, ALU.mult).then_inc(ps_free[g % 2], 1)
            normed_outputs(0)

            dve.wait_ge(tab_ld[1], 16)
            rotate(1, 0)
            rotate(1, 1)
            dve.wait_ge(rp_st, 16)
            dve.memset(state[:], 0.0).then_inc(s_upd, 1)
            with dve.Fori(0, NRC // 4) as i:
                for u in range(4):
                    c = i * 4 + u
                    chunk(1, c + NRC, c, u, i * 32 + (16 * (u // 2) + 16 + 16 * (DEC // 2)))
                    if u % 2:
                        t = u // 2
                        g = G_G[1] + t
                        dve.wait_ge(g_sg, i * 2 + (5 + t))
                        dve.tensor_copy(v1[:, :, bass.ds(c + (SEQ - 1), 2)],
                                        ps[:, 3 * (g % 2), CH + 8:CH + 16].rearrange("p (b t) -> p t b", b=2))
                        tile_ = t3(gbuf[:, bass.ds(i * 2 + t, 1), :].rearrange("p a n -> p (a n)"))
                        dve.tensor_tensor(tile_, pset(g), tile_, ALU.mult).then_inc(ps_free[g % 2], 1)
            normed_outputs(1)

            def merge(m, gs, ss):
                g = G_GB + 1
                dve.wait_ge(mm, ss + done(S_GB + 3))
                taken(dve, G_GB, gs)
                dve.wait_ge(mg_rdy, m + 1)
                dve.tensor_tensor(t3(gbuf[:, 1, :]), pset(g), t3(gbuf[:, 0, :]), ALU.mult
                                  ).then_inc(ps_free[g % 2], 1)
                taken(dve, g, gs)
                tile_ = ma[:, bass.ds(m, 1), :].rearrange("p a n -> p (a n)")
                dve.tensor_tensor(tile_, tile_, gbuf[:, 1, :], ALU.add).then_inc(mg_rdy, 1)

            def merged_lo(m):
                dve.wait_ge(mg_hi, m + 1)
                dve.tensor_tensor(mg_l[:, m, :], ma[:, m, :], mg_h[:, m, :].bitcast(F32), ALU.subtract
                                  ).then_inc(mg_lo, 1)

            with dve.Fori(0, KT - 1) as i:
                merge(i, i, i * 4)
            for m in range(4):
                merged_lo(m)
            merge(KT - 1, KT - 1, 4 * (KT - 1))
            for m in range(4, KT):
                merged_lo(m)

            dve.memset(gbuf[:, 3, :], 0.0).then_inc(wo_sum, 1)
            with dve.Fori(0, KT // 2) as i:
                for u in range(2):
                    dve.wait_ge(wo_sq, i * 2 + (u + 1))
                    dve.wait_ge(wo_sum, i * 2 + (u + 2))
                    dve.tensor_tensor(gbuf[:, 3, :], gbuf[:, 3, :], gbuf[:, 1 + u, :], ALU.add).then_inc(wo_sum, 1)

            dve.wait_ge(xa_ld, 16)
            for c in range(CHUNKS):
                cs = slice(c * CH, (c + 1) * CH)
                dve.wait_ge(m_rs, c + 1)
                dve.tensor_tensor(mix[:, :, cs], mix[:, :, cs],
                                  pch(G_MSTAT, c).unsqueeze(1).broadcast_to([P, KT, CH]), ALU.mult).then_inc(m_sc, 1)
                dve.wait_ge(m_sc, c + 1)
                dve.tensor_tensor(ma[:, 0:5, cs], mix[:, 0:5, cs], x_again[:, 0:5, cs], ALU.add
                                  ).then_inc(h_dve if c < CHUNKS - 1 else ps_free[G_MSTAT % 2], 1)
                dve.wait_ge(fx_hi, c + 1)
                for k in range(KT):
                    out = dve.scalar_tensor_tensor(fx_l[:, k, cs], ma[:, k, cs], vec[:, V_FPRE + k:V_FPRE + k + 1],
                                                   fx_h[:, k, cs].bitcast(F32), ALU.mult, ALU.subtract)
                out.then_inc(fx_lo, 1)
            dve.wait_ge(h_pool, CHUNKS)
            dve.memset(mix[:], 0.0).then_inc(f_zero, 1)
            dve.wait_ge(f_zero, 1)

            def hidden_lo(b, j, n):
                dve.wait_ge(hid_hi, n + 1)
                dve.tensor_tensor(hid_l[:, FB * (b % 2) + j, :], gbuf[:, 2 + j, :],
                                  hid_h[:, FB * (b % 2) + j, :].bitcast(F32), ALU.subtract).then_inc(hid_lo, 1)

            def add_down(m, g, ev, gshift=0):
                dve.wait_ge(mm, ev)
                taken(dve, g - 2, gshift)
                dve.tensor_tensor(t3(mix[:, m, :]), pset(g), t3(mix[:, m, :]), ALU.add
                                  ).then_inc(ps_free[g % 2], 1)

            def block_out(b, gs=0, es=0, hs=0):
                for j in range(FB):
                    hidden_lo(b + 1, j, hs + (2 * (b + 1) + j))
                for m in range(KT):
                    add_down(m, G_FFN + 4 + 10 * b + m, es + (E_FFN + PER_FB * b + 4 + m + 1), gs)

            for j in range(FB):
                hidden_lo(0, j, j)
            with dve.Fori(0, (NFB - 2) // 2) as i:
                block_out(0, i * 10, i * (2 * PER_FB), i * 4)
                block_out(1, i * 10, i * (2 * PER_FB), i * 4)
            dve.memset(hsum[:], 0.0).then_inc(h_sum, 1)
            b = NFB - 2
            for j in range(FB):
                hidden_lo(b + 1, j, 2 * (b + 1) + j)
            for m in range(KT):
                add_down(m, G_FFN + 4 + 10 * b + m, E_FFN + PER_FB * b + 4 + m + 1)
                dve.wait_ge(h_sq, m + 1)
                dve.wait_ge(h_sum, m + 1)
                dve.tensor_tensor(hsum[:], hsum[:], hsq[:], ALU.add).then_inc(h_sum, 1)
            dve.memset(gbuf[:, 3, :], 0.0).then_inc(f_sum, 1)

            def add_square(m):
                dve.wait_ge(f_sq, m + 1)
                dve.wait_ge(f_sum, m + 1)
                dve.tensor_tensor(gbuf[:, 3, :], gbuf[:, 3, :], gbuf[:, m % 2, :], ALU.add).then_inc(f_sum, 1)

            for m in range(KT):
                add_down(m, G_FSTAT - 8 + m, E_FFN + PER_FB * (NFB - 1) + m + 1)
                if m:
                    add_square(m - 1)
            add_square(KT - 1)

            for c in range(CHUNKS):
                cs = slice(c * CH, (c + 1) * CH)
                dve.wait_ge(f_st, c + 1)
                dve.wait_ge(h_ms, c + 1)
                dve.scalar_tensor_tensor(pch(G_FSTAT, c), pch(G_FSTAT, c), 1.0 / D_MODEL, hms[:, cs],
                                         ALU.mult, ALU.add).then_inc(f_den, 1)
            for c in range(CHUNKS):
                cs = slice(c * CH, (c + 1) * CH)
                dve.wait_ge(f_rs, c + 1)
                for k in reversed(range(KT)):
                    out = dve.scalar_tensor_tensor(mix[:, k, cs], mix[:, k, cs], vec[:, V_FPOST + k:V_FPOST + k + 1],
                                                   pch(G_FSTAT, c), ALU.mult, ALU.mult)
                out.then_inc(y_sc, 1)
                dve.wait_ge(y_sc, c + 1)
                dve.tensor_tensor(ma[:, 0:4, cs], mix[:, 0:4, cs], ma[:, 0:4, cs], ALU.add).then_inc(y_dve, 1)


def rope_tables():
    half = DK // 2
    steps = np.linspace(0.0, 1.0, half, dtype=np.float32).astype(np.float64)
    freqs = np.float32(1.0) / (ROPE_BASE ** steps).astype(np.float32)
    pos = np.concatenate([np.arange(SEQ), np.full(DEC, PAST_LEN)]).astype(np.float32)
    ang = (pos[None, :] * freqs[:, None]).astype(np.float32).astype(np.float64)
    place = np.where(np.arange(T) < SEQ, np.arange(T) % RC + 1, 0)
    out = np.empty((PAIRS, 2, half, 4, T), np.float64)
    for p in range(PAIRS):
        for h in range(2):
            decay = GAMMA[2 * p + h] ** place
            for w, factor in enumerate((decay, DK ** -0.5 / decay)):
                out[p, h, :, 2 * w] = np.cos(ang) * factor
                out[p, h, :, 2 * w + 1] = np.sin(ang) * factor
    return out.reshape(PAIRS, P, 4, T).astype(np.float32)


def weight_stream(w_in, w_conv, w_ret, w_o, w_up, w_down):
    n_val, n_gate, n_q, n_k = 0, CONV_DIM, 2 * CONV_DIM, 2 * CONV_DIM + HEADS * DK
    n_v = n_k + HEADS * DK
    n_g = n_v + HEADS * DV
    n_ga = n_g + HEADS * DV
    n_gb = n_ga + D_MODEL
    slots = []

    def put(w, ks, cols):
        slots.append(np.stack([w[k * P:(k + 1) * P, cols] for k in ks], axis=1))

    def put8(w, cols):
        put(w, range(4), cols)
        put(w, range(4, 8), cols)

    def run(start):
        return np.arange(start, start + P)

    for j in range(CT):
        put8(w_in, run(n_gate + j * P))
        put8(w_in, run(n_val + j * P))

    def qkv(p):
        half = DK // 2
        for base in (n_q, n_k):
            for part in range(2):
                put8(w_in, np.concatenate([base + (2 * p + h) * DK + part * half + np.arange(half) for h in range(2)]))
        for t in range(4):
            put8(w_in, run(n_v + (4 * p + t) * P))

    def gate(p):
        for t in range(4):
            put8(w_in, run(n_g + (4 * p + t) * P))

    qkv(0)
    gate(0)
    for m in range(KT):
        put8(w_in, run(n_ga + m * P))
    for m in range(KT):
        put(w_conv, range(4), run(m * P))
    qkv(1)
    gate(1)
    for m in range(KT):
        put8(w_in, run(n_gb + m * P))
        put8(w_ret, run(m * P))
    for m in range(KT):
        put8(w_o, run(m * P))

    def up(b):
        for j in range(FB):
            put8(w_up, run((FB * b + j) * P))

    def down(b):
        for m in range(0, KT, 2):
            slots.append(np.stack([w_down[(FB * b + k) * P:(FB * b + k + 1) * P, run((m + a) * P)]
                                   for a in range(2) for k in range(FB)], axis=1))

    up(0)
    for b in range(NFB):
        if b + 1 < NFB:
            up(b + 1)
        down(b)
    assert len(slots) == NSLOT
    return np.ascontiguousarray(np.stack(slots).reshape(NSLOT, P, SLOT))


def kernel(x_prompt, x_sample, cache_conv, state_ret, norm_mix_pre, norm_mix_post, w_in, w_dw, b_dw,
           conv_ln_w, conv_ln_b, w_conv_out, w_ret_out, w_o, norm_ffn_pre, norm_ffn_post, w_ffn_up,
           w_ffn_down):
    import concourse.bacc as bacc
    from concourse.bass_utils import run_bass_kernel_spmd

    def a(x):
        return np.asarray(x)

    x = np.concatenate([a(x_prompt)[0], a(x_sample)[:, 0]], axis=0)
    cols = [a(v)[0].reshape(-1, P).T for v in (norm_mix_pre, norm_mix_post, norm_ffn_pre, norm_ffn_post,
                                               conv_ln_w, conv_ln_b, b_dw)]
    history = np.zeros((P, CT, DEC, TAPS), np.float32)
    history[..., :HIST] = a(cache_conv)[0].reshape(DEC, HIST, CT, P).transpose(3, 2, 0, 1)
    ins = {
        "xT": x.T.reshape(KT, P, T).transpose(1, 0, 2),
        "wseq": weight_stream(a(w_in)[0], a(w_conv_out)[0], a(w_ret_out)[0], a(w_o)[0], a(w_ffn_up)[0],
                              a(w_ffn_down)[0]),
        "vecs": np.concatenate(cols, axis=1),
        "wdwT": a(w_dw)[0].reshape(TAPS, CT, P).transpose(2, 1, 0),
        "cacheT": history,
        "s_in": a(state_ret)[0],
        "rope": rope_tables(),
        "mask": np.triu(np.ones((RC, RC), np.float32)),
        "ident_in": np.eye(P, dtype=np.float32),
    }
    outs = {
        "yT": (P, KT, T),
        "convp": (P, CT, HIST),
        "convs": (P, CT, DEC, TAPS),
        "retp": (HEADS, DK, DV),
        "rets": (DEC, HEADS, DK, DV),
    }
    nc = bacc.Bacc("TRN2", target_bir_lowering=False, num_devices=1)
    ins = {name: np.ascontiguousarray(v) for name, v in ins.items()}
    args = [nc.dram_tensor(f"{name}_dram", v.shape, mybir.dt.from_np(v.dtype), kind="ExternalInput").ap()
            for name, v in ins.items()]
    args += [nc.dram_tensor(f"{name}_dram", shape, F32, kind="ExternalOutput").ap() for name, shape in outs.items()]
    build(nc, *args)
    r = run_bass_kernel_spmd(nc, [{f"{name}_dram": v for name, v in ins.items()}], core_ids=[0]).results[0]
    got = {name: np.asarray(r[f"{name}_dram"]) for name in outs}
    y = got["yT"].transpose(2, 1, 0).reshape(T, D_MODEL)
    return (y[:SEQ][None], y[SEQ:][:, None],
            got["convp"].transpose(2, 1, 0).reshape(1, 1, HIST, CONV_DIM),
            got["retp"][None, None],
            got["convs"][..., 1:].transpose(2, 3, 1, 0).reshape(1, DEC, HIST, CONV_DIM),
            got["rets"][None])
```

```python
from contextlib import ExitStack

import numpy as np

import concourse.bass as bass
from concourse import mybir

F32 = mybir.dt.float32
F32R = mybir.dt.float32r
ALU = mybir.AluOpType
ACT = mybir.ActivationFunctionType

P = 128
D_MODEL = 1024
SEQ = 1024
DEC = 8
T = SEQ + DEC
CHUNKS = 3
CH = T // CHUNKS
KT = D_MODEL // P
CONV_DIM = 512
CT = CONV_DIM // P
TAPS = 31
HIST = TAPS - 1
UW = HIST + T
HEADS = 4
PAIRS = HEADS // 2
DK = 128
DV = 256
RC = 128
NRC = SEQ // RC
FFN = 4096
EPS = 1e-6
PAST_LEN = 8192
ROPE_BASE = 10000.0
GAMMA = [1.0 - 2.0 ** (-5.0 - h) for h in range(HEADS)]

SLOT_TILES = 4
SLOT = SLOT_TILES * P
FB = 2
NFB = FFN // P // FB
RAW = 4
HL = 2

V_PRE, V_POST, V_FPRE, V_FPOST, V_LNW, V_LNB, V_BDW, NVEC = 0, 8, 16, 24, 32, 36, 40, 44

G_XSTAT = 0
G_U, S_U = 1, 0
G_QKV, S_QKV = [9, 39], [16, 64]
G_G, S_G = [17, 47], [32, 80]
G_GA, S_GA = 21, 40
G_LNM, G_LNV = 25, 27
G_AOUT, S_AOUT = 31, 56
G_GB, S_GB = 51, 88
G_WO, S_WO = 67, 120
G_WOB, S_WOB = 71, 128
G_FFN, S_FFN = 77, 136
G_LAST, S_LAST = 229, 260
LAST_TILES = ((0, 3), (3, 6), (6, 8))
NSLOT = 264


def build(nc, xT, wseq, vecs, wdwT, cacheT, s_in, rope, mask_d, ident_d,
          yT, convp, convs, retp, rets):
    vscr = nc.dram_tensor("v_sample_scratch", (PAIRS, DEC, 2 * DV), F32, kind="Internal").ap()

    with ExitStack() as ctx:
        at = [16512]

        def place(name, shape, dt=F32, offset=None):
            n = 4 * int(np.prod(shape[1:]))
            off = at[0] if offset is None else offset
            if offset is None:
                at[0] += -(-n // 32) * 32
            return nc.alloc_sbuf_tensor_at(name, list(shape), dt, offset=off), off

        def sem(name):
            return ctx.enter_context(nc.semaphore(name))

        xn_h, a_A = place("xn_h", [P, KT, T], F32R)
        xn_l, a_B = place("xn_l", [P, KT, T], F32R)
        u_ext, a_C1 = place("u_ext", [P, CT, UW])
        conv, a_C2 = place("conv", [P, CT, T])
        x_in, a_D = place("x_in", [P, KT, T])
        a_D2 = a_D + 4 * CT * T
        ma, a_E = place("ma", [P, KT, T])
        a_E2 = a_E + 4 * CT * T
        gbuf, a_G = place("gbuf", [P, 4, T])
        raw, _ = place("raw", [P, RAW, SLOT])
        w_h, _ = place("w_h", [P, HL, SLOT], F32R)
        w_l, _ = place("w_l", [P, HL, SLOT], F32R)
        mg_h, _ = place("mg_h", [P, KT, T], F32R, a_A)
        mg_l, _ = place("mg_l", [P, KT, T], F32R, a_B)
        fx_h, _ = place("fx_h", [P, KT, T], F32R, a_A)
        fx_l, _ = place("fx_l", [P, KT, T], F32R, a_B)
        wz_h, _ = place("wz_h", [P, 4, SLOT], F32R, a_A)
        wz_l, _ = place("wz_l", [P, 4, SLOT], F32R, a_B)
        fgain, _ = place("fgain", [P, 3, T], F32, a_A + 16 * SLOT)
        fsqB, _ = place("fsqB", [P, 3, 3 * CH], F32, a_B + 16 * SLOT)
        wc_h, _ = place("wc_h", [P, 2, SLOT], F32R, a_C2)
        wc_l, _ = place("wc_l", [P, 2, SLOT], F32R, a_C2 + 8 * SLOT)
        cv_h, _ = place("cv_h", [P, CT, UW], F32R, a_C1)
        cv_l, _ = place("cv_l", [P, CT, T], F32R, a_C2)
        qk1, _ = place("qk1", [P, 4, T], F32, a_C1)
        v1, _ = place("v1", [P, 4, T], F32, a_C2)
        ro1_h, _ = place("ro1_h", [P, 4, T], F32R, a_C1)
        ro1_l, _ = place("ro1_l", [P, 4, T], F32R, a_C2)
        h_res, _ = place("h_res", [P, KT, T], F32, a_C1)
        qk0, _ = place("qk0", [P, 4, T], F32, a_D)
        v0, _ = place("v0", [P, 4, T], F32, a_D2)
        ro0_h, _ = place("ro0_h", [P, 4, T], F32R, a_D)
        ro0_l, _ = place("ro0_l", [P, 4, T], F32R, a_D2)
        mix, _ = place("mix", [P, KT, T], F32, a_D)
        xsq, _ = place("xsq", [P, CHUNKS, KT * CH], F32, a_E)
        rope0, _ = place("rope0", [P, 4, T], F32, a_E)
        rtmp0, _ = place("rtmp0", [P, 4, CH], F32, a_E2)
        wo_h, _ = place("wo_h", [P, 8, SLOT], F32R, a_E)
        wo_l, _ = place("wo_l", [P, 8, SLOT], F32R, a_E + 32 * SLOT)
        hid_h, _ = place("hid_h", [P, 2 * FB, T], F32R, a_E)
        hid_l, _ = place("hid_l", [P, 2 * FB, T], F32R, a_E2)
        w1_h, _ = place("w1_h", [P, 2, SLOT], F32R, a_E + 12 * T)
        w1_l, _ = place("w1_l", [P, 2, SLOT], F32R, a_E2 + 12 * T)
        sgt, _ = place("sgt", [P, T], F32, a_G)
        hist, _ = place("hist", [P, CT, DEC, TAPS], F32, a_G + 4 * T)
        hprod, _ = place("hprod", [P, DEC, TAPS], F32, a_G + 8 * T)
        rope1, _ = place("rope1", [P, 4, T], F32, a_G)
        mask, _ = place("mask", [P, RC])
        ident, _ = place("ident", [P, P])
        ones, _ = place("ones", [P, P])
        vec, _ = place("vec", [P, NVEC])
        zero, _ = place("zero", [P, 1])
        eps_b, _ = place("eps_b", [P, 1])
        eps15_b, _ = place("eps15_b", [P, 1])
        qd_b, _ = place("qd_b", [P, 2, 2])
        kt_b, a_KT = place("kt_b", [P, 2, RC])
        vt_b, a_VT = place("vt_b", [P, 4, RC])
        p_b, _ = place("p_b", [P, 2, RC])
        state, _ = place("state", [P, 2, DV])
        s_dec, a_SS = place("s_dec", [P, 2, 2 * DV])
        v_bc, _ = place("v_bc", [P, 2 * DV])
        assert at[0] <= 229368, at[0]
        wdw, _ = place("wdw", [P, CT, TAPS], F32, a_VT)
        rtmp1, _ = place("rtmp1", [P, 4, CH], F32, a_SS)
        osq, _ = place("osq", [P, 2, 2 * CH], F32, a_SS)
        hsq, _ = place("hsq", [P, T], F32, a_KT)
        hsum, _ = place("hsum", [P, T], F32, a_SS)
        fsqA, _ = place("fsqA", [P, 3, 3 * CH], F32, a_G)
        hms, _ = place("hms", [P, T], F32, a_G + 12 * T)

        qk, vv = [qk0, qk1], [v0, v1]
        fsq = [fsqA, fsqB, fsqA]
        ro_h, ro_l = [ro0_h, ro1_h], [ro0_l, ro1_l]
        rtab, rtmp = [rope0, rope1], [rtmp0, rtmp1]

        ps = ctx.enter_context(nc.psum_tensor("ps", [P, 8, 512], F32))
        B6, B7 = ps[:, 6, :], ps[:, 7, :]

        def pset(g, n=CH):
            return ps[:, 3 * (g % 2):3 * (g % 2) + 3, 0:n]

        def pch(g, c):
            return ps[:, 3 * (g % 2) + c, 0:CH]

        def t3(ap):
            return ap.rearrange("p (c n) -> p c n", c=CHUNKS)

        x_ld = [sem(f"x_ld{c}") for c in range(CHUNKS)]
        cst_ld = sem("cst_ld")
        wdw_ld = sem("wdw_ld")
        hist_ld = sem("hist_ld")
        tab_ld = [sem("tab_ld0"), sem("tab_ld1")]
        raw_ld = [sem(f"raw_ld{i}") for i in range(RAW)]
        w_hi = sem("w_hi")
        w_split = sem("w_split")
        mm = sem("mm")
        ps_free = [sem("ps_free0"), sem("ps_free1")]
        c_init = sem("c_init")
        z_init = sem("z_init")
        x_sq = sem("x_sq")
        x_part = sem("x_part")
        x_one = sem("x_one")
        x_st = sem("x_st")
        x_ln = sem("x_ln")
        x_rs = sem("x_rs")
        x_sc = sem("x_sc")
        xn_hi = sem("xn_hi")
        xn_lo = sem("xn_lo")
        dve_c = sem("dve_c")
        cv_out = sem("cv_out")
        h_done = sem("h_done")
        cv_acc = sem("cv_acc")
        rope_p = sem("rope_p")
        rope_done = sem("rope_done")
        lnm_st = sem("lnm_st")
        lnv_st = sem("lnv_st")
        ln_xc = sem("ln_xc")
        ln_sq = sem("ln_sq")
        ln_ln = sem("ln_ln")
        ln_rs = sem("ln_rs")
        ln_n = sem("ln_n")
        ln_sg = sem("ln_sg")
        ln_z = sem("ln_z")
        ln_y = sem("ln_y")
        cv_hi = sem("cv_hi")
        cv_lo = sem("cv_lo")
        vs_T = sem("vs_T")
        vs_cp = sem("vs_cp")
        vs_st = sem("vs_st")
        staged = sem("staged")
        ret_a = sem("ret_a")
        vt_rdy = sem("vt_rdy")
        pk_rdy = sem("pk_rdy")
        ret_b = sem("ret_b")
        o_out = sem("o_out")
        s_upd = sem("s_upd")
        ss_ld = [sem("ss_ld0"), sem("ss_ld1")]
        ss_st = [sem("ss_st0"), sem("ss_st1")]
        vb_ld = sem("vb_ld")
        s_kv = sem("s_kv")
        s_new = sem("s_new")
        turns = sem("turns")
        g_sg = sem("g_sg")
        rp_st = sem("rp_st")
        on_sq = sem("on_sq")
        on_st = sem("on_st")
        on_ln = sem("on_ln")
        on_rs = sem("on_rs")
        on_n = sem("on_n")
        ro_g = sem("ro_g")
        ro_hi = sem("ro_hi")
        ro_lo = sem("ro_lo")
        mg_rdy = sem("mg_rdy")
        mg_hi = sem("mg_hi")
        mg_lo = sem("mg_lo")
        xa_ld = sem("xa_ld")
        wo_sq = sem("wo_sq")
        wo_sum = sem("wo_sum")
        m_st = sem("m_st")
        m_ln = sem("m_ln")
        m_rs = sem("m_rs")
        m_sc = sem("m_sc")
        h_dve = sem("h_dve")
        h_pool = sem("h_pool")
        fx_hi = sem("fx_hi")
        fx_lo = sem("fx_lo")
        hid_t = sem("hid_t")
        hid_hi = sem("hid_hi")
        hid_lo = sem("hid_lo")
        f_zero = sem("f_zero")
        h_sq = sem("h_sq")
        h_sum = sem("h_sum")
        h_st = sem("h_st")
        h_cp = sem("h_cp")
        f_den = sem("f_den")
        f_sq = sem("f_sq")
        f_gain = sem("f_gain")
        f_part = sem("f_part")
        f_sum = sem("f_sum")
        f_st = sem("f_st")
        f_ln = sem("f_ln")
        f_rs = sem("f_rs")
        y_sc = sem("y_sc")
        y_scp = sem("y_scp")
        y_dve = sem("y_dve")
        y_pool = sem("y_pool")
        y_st = sem("y_st")

        def done(slot):
            return slot + 1 + HL

        E_WOB = done(S_WOB - 1)
        E_FFN = E_WOB + 2 * CHUNKS + FB
        PER_FB = 2 * FB + KT
        E_LAST = E_FFN + PER_FB * (NFB - 1)

        def taken(e, g, shift=0):
            e.wait_ge(ps_free[g % 2], shift + (g // 2 + 1))

        def free_set(pe, g, shift=0):
            if g >= 2:
                taken(pe, g - 2, shift)

        YD = 5

        block = ctx.enter_context(nc.Block())

        @block.sync
        def _(sp):
            sp.dma_start(x_in[:, 0:4, 0:CH], xT[:, 0:4, 0:CH]).then_inc(x_ld[0], 16)
            sp.dma_start(x_in[:, :, CH:2 * CH], xT[:, :, CH:2 * CH]).then_inc(x_ld[1], 16)
            for s in range(RAW):
                sp.dma_start(raw[:, s, :], wseq[s]).then_inc(raw_ld[s], 16)
            sp.dma_start(x_in[:, :, 2 * CH:T], xT[:, :, 2 * CH:T]).then_inc(x_ld[2], 16)
            with sp.Fori(1, NSLOT // RAW) as i:
                for s in range(RAW):
                    sp.wait_ge(w_split, i * RAW + (s - RAW + 1))
                    sp.dma_start(raw[:, s, :], wseq[bass.ds(i * RAW + s, 1)].rearrange("a p n -> (a p) n")
                                 ).then_inc(raw_ld[s], 16)
            for c in range(CHUNKS):
                cs = slice(c * CH, (c + 1) * CH)
                sp.wait_ge(y_pool, c + 1)
                sp.dma_start(yT[:, YD:8, cs], h_res[:, YD:8, cs]).then_inc(y_st, 16)
                sp.wait_ge(y_dve, c + 1)
                sp.dma_start(yT[:, 0:YD, cs], h_res[:, 0:YD, cs]).then_inc(y_st, 16)
            sp.wait_ge(y_st, 16 * CHUNKS * 2)
            sp.wait_ge(cv_out, 16 * 2)
            sp.wait_ge(rp_st, 16 * PAIRS)
            for s in range(2):
                sp.wait_ge(ss_st[s], 16 + 16 * (DEC // 2) * PAIRS)
            sp.wait_ge(vs_st, 16 * PAIRS)

        @block.gpsimd
        def _(pool):
            pool.memset(zero[:], 0.0).then_inc(z_init, 1)
            pool.wait_ge(z_init, 1)

            def split(s, n, loads, used, hi=None, lo=None):
                hi = w_h[:, s % HL, :] if hi is None else hi
                lo = w_l[:, s % HL, :] if lo is None else lo
                pool.wait_ge(raw_ld[s], loads)
                if used is not None:
                    pool.wait_ge(mm, used)
                pool.tensor_tensor(hi, raw[:, s, :], zero[:, 0:1].broadcast_to([P, SLOT]), ALU.add
                                   ).then_inc(w_hi, 1)
                pool.wait_ge(w_hi, n + 1)
                pool.tensor_tensor(lo, raw[:, s, :], hi.bitcast(F32), ALU.subtract).then_inc(w_split, 1)

            split(0, 0, 16, 1)
            split(1, 1, 16, 2)
            for j in range(2):
                split(2 + j, 2 + j, 16, None, wc_h[:, j, :], wc_l[:, j, :])
            pool.wait_ge(x_sq, CHUNKS)
            for n in (4, 2):
                if n == 2:
                    pool.wait_ge(x_part, 1)
                pool.tensor_tensor(xsq[:, 2, 0:n * CH], xsq[:, 2, 0:n * CH], xsq[:, 2, n * CH:2 * n * CH],
                                   ALU.add).then_inc(x_part, 1)
            for s in range(RAW):
                split(s, RAW + s, 32, done(s) if s < HL else RAW + s + 1)
            with pool.Fori(2, S_WOB // RAW) as i:
                for s in range(RAW):
                    split(s, i * RAW + s, i * 16 + 16, i * RAW + (s + 1))
            pool.wait_ge(mg_hi, KT)
            pool.wait_ge(mg_lo, KT)
            for j in range(8):
                n = S_WOB + j
                split(j % RAW, n, 16 * (n // RAW) + 16, E_WOB - 3, wo_h[:, j, :], wo_l[:, j, :])
            for j in range(HL):
                split(j, S_FFN + j, 16 * (S_FFN // RAW) + 16, E_WOB - 1 + j)

            def add_x(c):
                cs = slice(c * CH, (c + 1) * CH)
                pool.wait_ge(m_sc, 2 * c + 2)
                pool.tensor_tensor(h_res[:, 4:8, cs], mix[:, 4:8, cs], h_res[:, 4:8, cs], ALU.add
                                   ).then_inc(h_pool, 1)

            pool.wait_ge(xa_ld, 16)
            add_x(0)
            add_x(1)
            for j in range(2):
                split(HL + j, S_FFN + HL + j, 16 * (S_FFN // RAW) + 16, E_WOB + 2 * CHUNKS,
                      w1_h[:, j, :], w1_l[:, j, :])
            add_x(2)
            for j, used in enumerate((-1, 0, 1, 2, 3, 4, 6, 8)):
                n = S_FFN + 4 + j
                split(j % RAW, n, 16 * (n // RAW) + 16, E_FFN + used)
            with pool.Fori(1, NFB - 1) as i:
                for j, used in enumerate((-2, 0, 1, 2, 3, 4, 6, 8)):
                    split(j % RAW, i * 8 + (S_FFN + 4 + j), i * 32 + 16 * ((S_FFN + 4 + j) // RAW + 1),
                          i * PER_FB + (E_FFN + used))
            for j in range(4):
                n = S_LAST + j
                split(j, n, 16 * (n // RAW) + 16, E_LAST - KT, wz_h[:, j, :], wz_l[:, j, :])

            def square_sum(c):
                pool.wait_ge(f_sq, 3 * c + 2)
                pool.tensor_tensor(fsq[c][:, 0, :], fsq[c][:, 0, :], fsq[c][:, 1, :], ALU.add).then_inc(f_part, 1)
                pool.wait_ge(f_sq, 3 * c + 3)
                pool.wait_ge(f_part, c + 1)
                pool.tensor_tensor(fsq[c][:, 0, 0:2 * CH], fsq[c][:, 0, 0:2 * CH], fsq[c][:, 2, 0:2 * CH],
                                   ALU.add).then_inc(f_sum, 1)

            def last_norm(c):
                cs = slice(c * CH, (c + 1) * CH)
                pool.wait_ge(f_gain, c + 1)
                pool.wait_ge(f_rs, c + 1)
                pool.tensor_tensor(fgain[:, :, cs], fgain[:, :, cs],
                                   hms[:, cs].unsqueeze(1).broadcast_to([P, KT - YD, CH]), ALU.mult
                                   ).then_inc(y_scp, 1)
                pool.wait_ge(y_scp, c + 1)
                pool.tensor_tensor(h_res[:, YD:8, cs], fgain[:, :, cs], h_res[:, YD:8, cs], ALU.add
                                   ).then_inc(y_pool, 1)

            square_sum(0)
            last_norm(0)
            square_sum(1)
            last_norm(1)
            last_norm(2)

        @block.tensor
        def _(pe):
            PARTS = ((0, 0), (0, 1), (1, 0))
            W = (w_h, w_l)
            XN = (xn_h, xn_l)
            pe.sem_inc(mm, HL)
            pe.sem_inc(ret_b, 1)

            def tile_mms(place_, sub, xs, k, g, first, last, chunks=range(CHUNKS), w=W):
                for n, (a, b) in enumerate(PARTS):
                    for c in chunks:
                        out = pe.matmul(pch(g, c), w[a][:, place_, sub * P:(sub + 1) * P],
                                        xs[b][:, k, c * CH:(c + 1) * CH],
                                        start=(first and n == 0), stop=(last and n == 2))
                return out

            def group8(g, slot, xs, gshift=0, sshift=0, between=None, before=None):
                free_set(pe, g, gshift)
                for half in range(2):
                    pe.wait_ge(w_split, sshift + (slot + half + 1))
                    for sub in range(SLOT_TILES):
                        k = SLOT_TILES * half + sub
                        if before:
                            before(k)
                        out = tile_mms((slot + half) % HL, sub, xs, k, g, k == 0, k == KT - 1)
                        if sub == SLOT_TILES - 1:
                            out.then_inc(mm, 1)
                        if between:
                            between(k)

            def stat_group(g, src, n, sem_):
                free_set(pe, g)
                for c in range(CHUNKS):
                    for j in range(n):
                        out = pe.matmul(pch(g, c), ones[:], src(j, c), start=(j == 0), stop=(j == n - 1))
                out.then_inc(sem_, 1)

            pe.wait_ge(c_init, 1)
            pe.wait_ge(x_one, 1)
            pe.matmul(pch(G_XSTAT, 0), ones[:], xsq[:, 0, 0:CH], start=True, stop=True).then_inc(x_st, 1)
            pe.wait_ge(x_sq, 2)
            for k in range(KT):
                out = pe.matmul(pch(G_XSTAT, 1), ones[:], xsq[:, 1, k * CH:(k + 1) * CH],
                                start=(k == 0), stop=(k == KT - 1))
            out.then_inc(x_st, 1)

            for c in range(CHUNKS):
                for t in range(2):
                    if c == 0:
                        pe.wait_ge(w_split, 2 * t + 2)
                    if t == 1 and c == 1:
                        pe.wait_ge(x_part, 2)
                        for k in range(2):
                            out = pe.matmul(pch(G_XSTAT, 2), ones[:], xsq[:, 2, k * CH:(k + 1) * CH],
                                            start=(k == 0), stop=(k == 1))
                        out.then_inc(x_st, 1)
                    for k in range(KT):
                        if t == 0:
                            pe.wait_ge(xn_hi, c * KT + k + 1)
                            pe.wait_ge(xn_lo, c * KT + k + 1)
                        out = tile_mms(k // SLOT_TILES, k % SLOT_TILES, XN, k, G_U + t, k == 0, k == KT - 1,
                                       (c,), (wc_h, wc_l) if t else W)
                        if c == CHUNKS - 1 and k % SLOT_TILES == SLOT_TILES - 1:
                            out.then_inc(mm, 1)
            with pe.Fori(0, CT - 1) as i:
                group8(G_U + 2, S_U + 4, XN, i, i * 4)
                group8(G_U + 3, S_U + 6, XN, i, i * 4)

            def qkv(p, between=None):
                group8(G_QKV[p], S_QKV[p], XN, between=between)
                group8(G_QKV[p] + 1, S_QKV[p] + 2, XN)
                with pe.Fori(0, 3) as i:
                    group8(G_QKV[p] + 2, S_QKV[p] + 4, XN, i, i * 4)
                    group8(G_QKV[p] + 3, S_QKV[p] + 6, XN, i, i * 4)

            def v_decode(p):
                if p:
                    pe.wait_ge(on_n, 6)
                for t in range(4):
                    out = pe.transpose(ps[0:DEC, 7, t * P:(t + 1) * P], vv[p][:, t, SEQ:T], ident[:])
                out.then_inc(vs_T, 1)

            def chunk_a(p, n, col):
                pe.wait_ge(staged, n * 2 + 2)
                pe.wait_ge(o_out, n + 1)
                pe.wait_ge(s_upd, n + (p + 1))
                for h in range(2):
                    pe.matmul(B6[:, h * RC:(h + 1) * RC], kt_b[:, h, :], qk[p][:, h, bass.ds(col, RC)],
                              start=True, stop=True)
                for h in range(2):
                    pe.transpose(B6[:, (2 + h) * RC:(3 + h) * RC], kt_b[:, h, :], ident[:])
                for t in range(4):
                    out = pe.transpose(B7[:, t * RC:(t + 1) * RC], vt_b[:, t, :], ident[:])
                out.then_inc(ret_a, 1)

            def chunk_b(p, n, col):
                pe.wait_ge(vt_rdy, n + 1)
                pe.wait_ge(pk_rdy, n * 3 + 3)
                for h in range(2):
                    for e in range(2):
                        o = B6[:, (2 * h + e) * RC:(2 * h + e + 1) * RC]
                        pe.matmul(o, vt_b[:, 2 * h + e, :], p_b[:, h, :], start=True, stop=False)
                        pe.matmul(o, state[:, h, e * P:(e + 1) * P], qk[p][:, h, bass.ds(col, RC)],
                                  start=False, stop=True)
                for h in range(2):
                    out = pe.matmul(B7[:, h * DV:(h + 1) * DV], kt_b[:, h, :],
                                    vt_b[:, 2 * h:2 * h + 2, :].rearrange("p a n -> p (a n)"),
                                    start=True, stop=True)
                out.then_inc(ret_b, 1)

            def decode_out(g, j, u, n):
                pe.wait_ge(s_new, n + 2)
                for h in range(2):
                    for e in range(2):
                        at_ = CH + 8 + 4 * j + 2 * h + e
                        out = pe.matmul(ps[:, 3 * (g % 2), at_:at_ + 1],
                                        s_dec[:, u % 2, h * DV + e * P:h * DV + (e + 1) * P],
                                        qd_b[:, u % 2, h:h + 1], start=True, stop=True)
                return out

            def ret_slot(p, g, slot, xs, k0, ktiles, u, c, gshift, sshift):
                n = c + NRC * p
                if k0 == 0:
                    free_set(pe, g, gshift)
                pe.wait_ge(w_split, sshift + (slot + 1))
                for half in range(2):
                    for sub in (2 * half, 2 * half + 1):
                        k = k0 + sub
                        out = tile_mms(slot % HL, sub, xs, k, g, k == 0, k == ktiles - 1)
                    if half == 0:
                        chunk_a(p, n, c * RC)
                    else:
                        last = out
                return last, n

            qkv(0)
            with pe.Fori(0, 2) as i:
                group8(G_G[0], S_G[0], XN, i, i * 4)
                group8(G_G[0] + 1, S_G[0] + 2, XN, i, i * 4)

            with pe.Fori(0, 2) as i:
                group8(G_GA, S_GA, XN, i, i * 4)
                group8(G_GA + 1, S_GA + 2, XN, i, i * 4)
            pe.wait_ge(cv_acc, 2 * TAPS * CT)
            pe.wait_ge(h_done, 2 * CT)
            stat_group(G_LNM, lambda j, c: conv[:, j, c * CH:(c + 1) * CH], CT, lnm_st)
            v_decode(0)
            group8(G_LNM + 1, S_GA + 8, XN)
            pe.wait_ge(ln_sq, CT)
            stat_group(G_LNV, lambda j, c: u_ext[:, j, c * CH:(c + 1) * CH], CT, lnv_st)
            for j in range(3):
                group8(G_LNV + 1 + j, S_GA + 10 + 2 * j, XN)

            pe.wait_ge(cv_hi, CT)
            pe.wait_ge(cv_lo, CT)
            pe.wait_ge(rope_done, 2 * CHUNKS)
            with pe.Fori(0, NRC // 2) as i:
                for u in range(2):
                    g = G_AOUT + u
                    c = i * 2 + u
                    out, n = ret_slot(0, g, S_AOUT + u, (cv_h, cv_l), 0, CT, u, c, i, i * 2)
                    chunk_b(0, n, c * RC)
                    decode_out(g, 0, u, n).then_inc(mm, 1)

            def out_stats(p):
                def between(k):
                    i = k - 1
                    if not 0 <= i < 2 * CHUNKS:
                        return
                    pe.wait_ge(on_sq, 6 * p + i + 1)
                    if i == 0:
                        pe.wait_ge(o_out, NRC * (p + 1) + 1)
                    elif i == 1:
                        pe.wait_ge(s_upd, (1 + NRC) * (p + 1))
                    else:
                        pe.wait_ge(on_n, 6 * p + i - 1)
                    for e in range(2):
                        out = pe.matmul(ps[:, 6 + i % 2, 0:CH], ones[:], osq[:, i % 2, e * CH:(e + 1) * CH],
                                        start=(e == 0), stop=(e == 1))
                    out.then_inc(on_st, 1)
                return between

            qkv(1, out_stats(0))
            pe.wait_ge(rope_done, 4 * CHUNKS)
            taken(pe, G_QKV[1] + 7)
            v_decode(1)
            with pe.Fori(0, 2) as i:
                for t in range(2):
                    g = G_G[1] + t
                    for half in range(2):
                        u = 2 * t + half
                        c = i * 4 + u
                        out, n = ret_slot(1, g, S_G[1] + u, XN, 4 * half, KT, u, c, i, i * 4)
                        if half == 0:
                            out.then_inc(mm, 1)
                        chunk_b(1, n, c * RC)
                    for j in range(2):
                        last = decode_out(g, j, j, n - 1 + j)
                    last.then_inc(mm, 1)

            def b_out(gs=0, ss=0, wait=False):
                g, slot = G_GB + 1, S_GB + 2
                free_set(pe, g, gs)
                for half in range(2):
                    if wait:
                        pe.wait_ge(ro_hi, 4 * half + 4)
                        pe.wait_ge(ro_lo, 4 * half + 4)
                    pe.wait_ge(w_split, ss + (slot + half + 1))
                    for sub in range(SLOT_TILES):
                        out = tile_mms((slot + half) % HL, sub, (ro_h[half], ro_l[half]), sub, g,
                                       half == 0 and sub == 0, half == 1 and sub == 3)
                    out.then_inc(mm, 1)

            group8(G_GB, S_GB, XN, between=out_stats(1))
            b_out(wait=True)
            with pe.Fori(1, KT) as i:
                group8(G_GB, S_GB, XN, i, i * 4)
                b_out(i, i * 4)

            MG = (mg_h, mg_l)

            def merged(k):
                pe.wait_ge(mg_hi, k + 1)
                pe.wait_ge(mg_lo, k + 1)

            group8(G_WO, S_WO, MG, before=merged)
            group8(G_WO + 1, S_WO + 2, MG)
            group8(G_WO + 2, S_WO + 4, MG)
            group8(G_WO + 3, S_WO + 6, MG)

            def mix_stat(c):
                pe.wait_ge(wo_sum, 6 + 4 * (c + 1))
                if c == 0:
                    pe.wait_ge(on_n, 12)
                if c == 2:
                    pe.wait_ge(m_sc, 2)
                pe.matmul(ps[:, 6 + c % 2, 0:CH], ones[:], gbuf[:, 3, c * CH:(c + 1) * CH],
                          start=True, stop=True).then_inc(m_st, 1)

            for c in range(CHUNKS):
                for half in range(2):
                    g = G_WOB + 2 * c + half
                    free_set(pe, g)
                    for m in range(2):
                        for k in range(KT):
                            slot = 4 * half + 2 * m + k // SLOT_TILES
                            if c == 0 and k % SLOT_TILES == 0:
                                pe.wait_ge(w_split, S_WOB + slot + 1)
                            for n, (a, b) in enumerate(PARTS):
                                sub = k % SLOT_TILES
                                out = pe.matmul(pch(g, m), (wo_h, wo_l)[a][:, slot, sub * P:(sub + 1) * P],
                                                MG[b][:, k, c * CH:(c + 1) * CH],
                                                start=(k == 0 and n == 0), stop=(k == KT - 1 and n == 2))
                    out.then_inc(mm, 1)
                    if half == 0 and c > 0:
                        mix_stat(c - 1)

            FX = (fx_h, fx_l)
            HID = (hid_h, hid_l)
            for c, j in ((0, 0), (1, 0), (0, 1), (1, 1), (2, 0), (2, 1)):
                g = G_FFN + j
                if c == 0:
                    free_set(pe, g)
                for k in range(KT):
                    if c == 0 and k % SLOT_TILES == 0:
                        pe.wait_ge(w_split, S_FFN + 2 * j + k // SLOT_TILES + 1)
                    if j == 0:
                        pe.wait_ge(fx_hi, c * KT + k + 1)
                        pe.wait_ge(fx_lo, c * KT + k + 1)
                    out = tile_mms(k // SLOT_TILES, k % SLOT_TILES, FX, k, g, k == 0, k == KT - 1, (c,),
                                   W if j == 0 else (w1_h, w1_l))
                if c == 2:
                    out.then_inc(mm, 1)
                if (c, j) == (0, 0):
                    mix_stat(2)

            def down(b, g, slot, gshift, sshift, hshift):
                pe.wait_ge(hid_hi, hshift + 2 * (b + 1))
                pe.wait_ge(hid_lo, hshift + (2 * (b + 1) + 2))
                for m in range(KT):
                    free_set(pe, g + m, gshift)
                    if m % 2 == 0:
                        pe.wait_ge(w_split, sshift + (slot + m // 2 + 1))
                    for k in range(FB):
                        out = tile_mms((slot + m // 2) % HL, FB * (m % 2) + k, HID, FB * (b % 2) + k,
                                       g + m, k == 0, k == FB - 1)
                    out.then_inc(mm, 1)

            def up_down(b, gshift=0, sshift=0, hshift=0):
                g, slot = G_FFN + 2 + 10 * b, S_FFN + 4 + 8 * b
                group8(g, slot, FX, gshift, sshift)
                group8(g + 1, slot + 2, FX, gshift, sshift)
                down(b, g + 2, slot + 4, gshift, sshift, hshift)

            with pe.Fori(0, (NFB - 2) // 2) as i:
                up_down(0, i * 10, i * 16, i * 4)
                up_down(1, i * 10, i * 16, i * 4)
            up_down(NFB - 2)
            pe.wait_ge(h_sum, KT + 1)
            for c in range(CHUNKS):
                if c == 2:
                    pe.wait_ge(h_cp, 1)
                pe.matmul(ps[:, 6 + c % 2, 0:CH], ones[:], hsum[:, c * CH:(c + 1) * CH],
                          start=True, stop=True).then_inc(h_st, 1)

            def out_stat(c):
                pe.wait_ge(f_sum, c + 1)
                pe.wait_ge(h_cp, CHUNKS)
                if c == 2:
                    pe.wait_ge(f_rs, 1)
                bank = ps[:, 6 + c % 2, 0:CH]
                for q in range(3):
                    out = pe.matmul(bank, ones[:], fsq[c][:, 0, q * CH:(q + 1) * CH],
                                    start=(q == 0), stop=(q == 2 and c < 2))
                if c == 2:
                    pe.wait_ge(f_sq, 3 * CHUNKS)
                    for q in range(2):
                        out = pe.matmul(bank, ones[:], fsq[c][:, 2, q * CH:(q + 1) * CH],
                                        start=False, stop=(q == 1))
                out.then_inc(f_st, 1)

            pe.wait_ge(hid_hi, 2 * NFB)
            pe.wait_ge(hid_lo, 2 * NFB + 2)
            for c in range(CHUNKS):
                for q, (m0, m1) in enumerate(LAST_TILES):
                    g = G_LAST + 3 * c + q
                    free_set(pe, g)
                    for m in range(m0, m1):
                        if c == 0:
                            pe.wait_ge(w_split, S_LAST + m // 2 + 1)
                        for k in range(FB):
                            sub = FB * (m % 2) + k
                            for n, (a, b) in enumerate(PARTS):
                                out = pe.matmul(pch(g, m - m0), (wz_h, wz_l)[a][:, m // 2, sub * P:(sub + 1) * P],
                                                HID[b][:, FB * ((NFB - 1) % 2) + k, c * CH:(c + 1) * CH],
                                                start=(k == 0 and n == 0), stop=(k == FB - 1 and n == 2))
                    out.then_inc(mm, 1)
                    if q == 1 and c > 0:
                        out_stat(c - 1)
            out_stat(CHUNKS - 1)

        @block.scalar
        def _(act):
            def rsqrt_mean(src, n, ln_sem, rs_sem, count):
                act.activation(src, src, ACT.Ln, bias=eps_b[:], scale=1.0 / n).then_inc(ln_sem, 1)
                act.wait_ge(ln_sem, count)
                return act.activation(src, src, ACT.Exp, scale=-0.5).then_inc(rs_sem, 1)

            act.dma_start(x_in[:, 4:8, 0:CH], xT[:, 4:8, 0:CH]).then_inc(x_ld[0], 16)
            act.preload_act_table_set("natural_log_exp_and_others")
            act.dma_start(vec[:], vecs).then_inc(cst_ld, 16)
            act.dma_start(ident[:], ident_d).then_inc(cst_ld, 16)
            act.dma_start(mask[:], mask_d).then_inc(cst_ld, 16)
            act.dma_start(wdw[:], wdwT).then_inc(wdw_ld, 16)
            act.dma_start(hist[:], cacheT).then_inc(hist_ld, 16)
            act.sem_inc(o_out, 1)
            act.sem_inc(ss_st[0], 16)
            act.sem_inc(ss_st[1], 16)

            def x_square(c):
                act.wait_ge(x_ld[c], 16 if c else 32)
                n = KT if c else KT // 2
                act.activation(xsq[:, c, 0:n * CH].rearrange("p (k n) -> p k n", k=n),
                               x_in[:, 0:n, c * CH:(c + 1) * CH], ACT.Square).then_inc(x_sq, 1)

            def x_rms(c):
                act.wait_ge(x_st, c + 1)
                rsqrt_mean(pch(G_XSTAT, c), D_MODEL, x_ln, x_rs, c + 1)

            def x_hi(c):
                if c == 0:
                    act.wait_ge(cst_ld, 48)
                for k in range(KT):
                    if k % 4 == 0:
                        half = 2 * c + k // 4
                        if half < 2 * CHUNKS - 1:
                            act.wait_ge(x_sc, half + 1)
                        else:
                            taken(act, G_XSTAT)
                    act.activation(xn_h[:, k, c * CH:(c + 1) * CH], x_in[:, k, c * CH:(c + 1) * CH],
                                   ACT.Copy, scale=vec[:, V_PRE + k:V_PRE + k + 1]).then_inc(xn_hi, 1)

            x_square(0)
            x_square(1)
            act.wait_ge(c_init, 3)
            x_rms(0)
            x_hi(0)
            x_rms(1)
            x_square(2)
            x_hi(1)
            x_rms(2)
            x_hi(2)

            act.wait_ge(x_st, CHUNKS)
            act.dma_start(rope0[:], rope[0]).then_inc(tab_ld[0], 16)

            for j in range(CT):
                g = G_U + 2 * j
                act.wait_ge(mm, done(S_U + 4 * j + 1))
                if j:
                    taken(act, g - 1)
                act.activation(t3(sgt[:]), pset(g), ACT.Sigmoid).then_inc(ps_free[g % 2], 1)

            def qkv_out(p):
                for t in range(8):
                    g = G_QKV[p] + t
                    act.wait_ge(mm, done(S_QKV[p] + 2 * t + 1))
                    if t == 0 and p == 0:
                        act.wait_ge(xn_lo, CHUNKS * KT)
                    if t >= 4:
                        act.wait_ge(rope_done, 2 * CHUNKS * p + CHUNKS * (1 + (t - 4) // 2))
                    act.activation(t3(vv[p][:, t % 4, :]), pset(g), ACT.Copy).then_inc(ps_free[g % 2], 1)

            qkv_out(0)
            act.wait_ge(h_done, 2 * CT)
            act.dma_start(convp, u_ext[:, :, SEQ:SEQ + HIST]).then_inc(cv_out, 16)
            act.dma_start(convs, hist[:]).then_inc(cv_out, 16)
            act.wait_ge(cv_out, 32)
            for t in range(4):
                g = G_G[0] + t
                act.wait_ge(mm, done(S_G[0] + 2 * t + 1))
                act.activation(t3(gbuf[:, t, :]), pset(g), ACT.Sigmoid).then_inc(g_sg, 1)

            def ga_out(m):
                g = G_GA + m + (m >= 4) + (m >= 5)
                act.wait_ge(mm, done(S_GA + 2 * m + 1))
                act.activation(t3(ma[:, m, :]), pset(g), ACT.Sigmoid).then_inc(ps_free[g % 2], 1)

            act.wait_ge(rope_done, 2 * CHUNKS)
            for m in range(4):
                ga_out(m)
            act.preload_act_table_set("natural_log_exp_and_others")
            for j in range(CT):
                if j < CT - 1:
                    act.wait_ge(ln_xc, j + 1)
                else:
                    taken(act, G_LNM)
                act.activation(u_ext[:, j, 0:T], conv[:, j, :], ACT.Square).then_inc(ln_sq, 1)

            def v_decode_out(p):
                act.wait_ge(vs_T, p + 1)
                act.activation(vt_b[0:DEC].rearrange("p a n -> p (a n)"), ps[0:DEC, 7, :],
                               ACT.Copy).then_inc(vs_cp, 1)
                act.wait_ge(vs_cp, p + 1)
                act.dma_start(vscr[p], vt_b[0:DEC].rearrange("p a n -> p (a n)")).then_inc(vs_st, 16)

            v_decode_out(0)
            act.wait_ge(mm, done(S_GA + 9))
            act.activation(t3(ma[:, 4, :]), pset(G_LNM + 1), ACT.Copy).then_inc(ps_free[(G_LNM + 1) % 2], 1)
            act.wait_ge(lnv_st, 1)
            rsqrt_mean(pset(G_LNV), CONV_DIM, ln_ln, ln_rs, 1)
            for j in range(CT):
                if j < CT - 1:
                    act.wait_ge(ln_n, j + 1)
                else:
                    taken(act, G_LNV)
                act.activation(u_ext[:, j, 0:T], conv[:, j, :], ACT.Sigmoid,
                               bias=vec[:, V_LNB + j:V_LNB + j + 1],
                               scale=vec[:, V_LNW + j:V_LNW + j + 1]).then_inc(ln_sg, 1)
            taken(act, G_LNM + 1)
            act.activation(ma[:, 4, :], ma[:, 4, :], ACT.Sigmoid)
            for j in range(CT):
                act.wait_ge(ln_y, j + 1)
                act.activation(cv_h[:, j, 0:T], conv[:, j, :], ACT.Copy).then_inc(cv_hi, 1)
            for m in range(5, KT):
                ga_out(m)

            def chunk_io(p, n, b, u, pe_done):
                act.wait_ge(ret_b, n + 1)
                act.sem_inc(turns, 1)
                act.activation(kt_b[:], qk[p][:, 2:4, bass.ds(b * RC, RC)], ACT.Copy).then_inc(staged, 1)
                act.activation(vt_b[:], vv[p][:, :, bass.ds(b * RC, RC)], ACT.Copy).then_inc(staged, 1)
                w = u % 2
                act.wait_ge(ss_st[w], pe_done[1])
                act.wait_ge(mm, pe_done[0])
                act.dma_start(s_dec[:, w, :].rearrange("p (h e) -> p h e", h=2),
                              s_in[bass.ds(b, 1), 2 * p:2 * p + 2].rearrange("a h p e -> p (a h) e")
                              ).then_inc(ss_ld[w], 16)
                act.wait_ge(s_new, n + 1)
                act.dma_start(v_bc[:], vscr[p, bass.ds(b, 1), :].broadcast_to([P, 2 * DV])
                              ).then_inc(vb_ld, 16)

            def chunk_out(p, n, b, u):
                act.wait_ge(ret_a, n + 1)
                act.activation(vt_b[:], B7.rearrange("p (a n) -> p a n", a=4), ACT.Copy).then_inc(vt_rdy, 1)
                act.wait_ge(ret_b, n + 2)
                act.sem_inc(turns, 1)
                act.activation(vv[p][:, :, bass.ds(b * RC, RC)], B6.rearrange("p (a n) -> p a n", a=4),
                               ACT.Copy).then_inc(o_out, 1)
                act.wait_ge(s_new, n + 2)
                act.dma_start(rets[bass.ds(b, 1), 2 * p:2 * p + 2].rearrange("a h p e -> p (a h) e"),
                              s_dec[:, u % 2, :].rearrange("p (h e) -> p h e", h=2)
                              ).then_inc(ss_st[u % 2], 16)

            def ret_tail(p, last_group):
                act.wait_ge(s_upd, (1 + NRC) * (p + 1))
                act.dma_start(retp[2 * p:2 * p + 2].rearrange("h p e -> p h e"),
                              state[:]).then_inc(rp_st, 16)
                taken(act, last_group)
                for w in range(2):
                    act.wait_ge(ss_st[w], 16 + 16 * (DEC // 2) * (p + 1))
                def square(i):
                    if 6 * p + i >= 2:
                        act.wait_ge(on_st, 6 * p + i - 1)
                    h, c = divmod(i, CHUNKS)
                    act.activation(osq[:, i % 2, :].rearrange("p (a n) -> p a n", a=2),
                                   vv[p][:, 2 * h:2 * h + 2, c * CH:(c + 1) * CH], ACT.Square).then_inc(on_sq, 1)

                act.preload_act_table_set("natural_log_exp_and_others")
                square(0)
                square(1)
                for i in range(2 * CHUNKS):
                    act.wait_ge(on_st, 6 * p + i + 1)
                    rsqrt_mean(ps[:, 6 + i % 2, 0:CH], DV, on_ln, on_rs, 6 * p + i + 1)
                    if i + 2 < 2 * CHUNKS:
                        square(i + 2)
                for t in range(4):
                    act.wait_ge(ro_g, 4 * p + t + 1)
                    act.activation(ro_h[p][:, t, :], vv[p][:, t, :], ACT.Copy).then_inc(ro_hi, 1)
                if p:
                    act.preload_act_table_set("sigmoid_and_others")

            act.wait_ge(rope_done, 2 * CHUNKS)
            act.wait_ge(vs_st, 16)
            with act.Fori(0, NRC // 2) as i:
                for u in range(2):
                    c = i * 2 + u
                    chunk_io(0, c, c, u, (i * 2 + (done(S_AOUT) + u - 2), i * 16 + 16))
                    chunk_out(0, c, c, u)
            ret_tail(0, G_AOUT + 7)

            act.wait_ge(ro_g, 4)
            act.dma_start(rope1[:], rope[1]).then_inc(tab_ld[1], 16)
            qkv_out(1)
            v_decode_out(1)
            act.wait_ge(rope_done, 4 * CHUNKS)
            act.wait_ge(vs_st, 32)
            act.preload_act_table_set("sigmoid_and_others")
            with act.Fori(0, NRC // 4) as i:
                for u in range(4):
                    c = i * 4 + u
                    n = c + NRC
                    chunk_io(1, n, c, u, (i * 4 + (done(S_G[1]) - 1 + 2 * (u // 2)),
                                          i * 32 + (16 * (u // 2) + 16 + 16 * (DEC // 2))))
                    chunk_out(1, n, c, u)
                    if u % 2:
                        t = u // 2
                        act.wait_ge(mm, i * 4 + done(S_G[1] + 2 * t + 1))
                        act.sem_inc(turns, 1)
                        act.activation(t3(gbuf[:, bass.ds(i * 2 + t, 1), :].rearrange("p a n -> p (a n)")),
                                       pset(G_G[1] + t), ACT.Sigmoid).then_inc(g_sg, 1)
            ret_tail(1, G_G[1] + 3)

            def gb_out(gs, ss):
                act.wait_ge(mm, ss + done(S_GB + 1))
                taken(act, G_GB - 1, gs)
                act.activation(t3(gbuf[:, 0, :]), pset(G_GB), ACT.Sigmoid).then_inc(ps_free[G_GB % 2], 1)

            act.wait_ge(ro_lo, 8)
            with act.Fori(0, KT - 1) as i:
                gb_out(i, i * 4)
            gb_out(KT - 1, 4 * (KT - 1))
            for m in range(KT):
                act.wait_ge(mg_rdy, m + 2)
                act.activation(mg_h[:, m, :], ma[:, m, :], ACT.Copy).then_inc(mg_hi, 1)
            act.wait_ge(mm, done(S_WO - 1))
            act.dma_start(h_res[:], xT).then_inc(xa_ld, 16)

            act.preload_act_table_set("natural_log_exp_and_others")
            with act.Fori(0, 2) as i:
                for u in range(2):
                    g = G_WO + u
                    act.wait_ge(mm, i * 4 + done(S_WO + 2 * u + 1))
                    act.wait_ge(wo_sum, i * 2 + (u + 1))
                    act.activation(t3(gbuf[:, 1 + u, :]), pset(g), ACT.Square).then_inc(wo_sq, 1)
                    act.activation(t3(mix[:, bass.ds(i * 2 + u, 1), :].rearrange("p a n -> p (a n)")),
                                   pset(g), ACT.Copy,
                                   scale=vec[:, bass.ds(i * 2 + (V_POST + u), 1)]).then_inc(ps_free[g % 2], 1)

            def wob_out(c, half):
                j = 2 * c + half
                g = G_WOB + j
                act.wait_ge(mm, E_WOB + j + 1)
                act.wait_ge(wo_sum, 5 + j if j < 2 else 6 + 2 * (j - 1))
                banks = ps[:, 3 * (g % 2):3 * (g % 2) + 2, 0:CH]
                act.activation(gbuf[:, 1 + half, 0:2 * CH].rearrange("p (a n) -> p a n", a=2), banks,
                               ACT.Square).then_inc(wo_sq, 1)
                for m in range(2):
                    k = 4 + 2 * half + m
                    out = act.activation(mix[:, k, c * CH:(c + 1) * CH], pch(g, m), ACT.Copy,
                                         scale=vec[:, V_POST + k:V_POST + k + 1])
                out.then_inc(ps_free[g % 2], 1)

            def m_rms(c):
                act.wait_ge(m_st, c + 1)
                rsqrt_mean(ps[:, 6 + c % 2, 0:CH], D_MODEL, m_ln, m_rs, c + 1)

            def fx_hi_part(c):
                for k in range(KT):
                    if k == 0:
                        act.wait_ge(h_dve, c + 1)
                    if k == 4:
                        act.wait_ge(h_pool, c + 1)
                    act.activation(fx_h[:, k, c * CH:(c + 1) * CH], h_res[:, k, c * CH:(c + 1) * CH],
                                   ACT.Copy, scale=vec[:, V_FPRE + k:V_FPRE + k + 1]).then_inc(fx_hi, 1)

            wob_out(0, 0)
            wob_out(0, 1)
            wob_out(1, 0)
            m_rms(0)
            wob_out(1, 1)
            wob_out(2, 0)
            m_rms(1)
            wob_out(2, 1)
            fx_hi_part(0)
            fx_hi_part(1)
            m_rms(2)
            fx_hi_part(2)

            def up_out(g, b, j, ev, n, gshift=0):
                act.wait_ge(mm, ev)
                act.activation(t3(gbuf[:, j, :]), pset(g), ACT.Relu).then_inc(ps_free[g % 2], 1)
                taken(act, g, gshift)
                act.wait_ge(hid_lo, n + 1)
                act.activation(gbuf[:, 2 + j, :], gbuf[:, j, :], ACT.Square).then_inc(hid_t, 1)
                act.activation(hid_h[:, FB * (b % 2) + j, :], gbuf[:, j, :], ACT.Square).then_inc(hid_hi, 1)

            for j in range(FB):
                up_out(G_FFN + j, 0, j, E_FFN - 1 + j, j)
            with act.Fori(0, (NFB - 2) // 2) as i:
                for v in range(2):
                    for j in range(FB):
                        up_out(G_FFN + 2 + 10 * v + j, v + 1, j, i * (2 * PER_FB) + (E_FFN + PER_FB * v + 2 * (j + 1)),
                               i * 4 + (2 * (v + 1) + j), i * 10)
                act.wait_ge(h_sum, i + 1)
                act.sem_inc(turns, 1)
                act.activation(hsq[:], h_res[:, bass.ds(i, 1), :].rearrange("p a n -> p (a n)"), ACT.Square
                               ).then_inc(h_sq, 1)
            act.wait_ge(h_sum, KT)
            act.activation(hsq[:], h_res[:, KT - 1, :], ACT.Square).then_inc(h_sq, 1)
            b = NFB - 1
            for j in range(FB):
                up_out(G_FFN + 2 + 10 * (b - 1) + j, b, j, E_FFN + PER_FB * (b - 1) + 2 * (j + 1), 2 * b + j)

            for c in range(CHUNKS):
                act.wait_ge(h_st, c + 1)
                act.activation(hms[:, c * CH:(c + 1) * CH], ps[:, 6 + c % 2, 0:CH], ACT.Square,
                               bias=eps15_b[:], scale=EPS ** 0.5 / D_MODEL).then_inc(h_cp, 1)

            def f_rms(c):
                act.wait_ge(f_den, c + 1)
                bank = ps[:, 6 + c % 2, 0:CH]
                act.activation(bank, bank, ACT.Ln).then_inc(f_ln, 1)
                act.wait_ge(f_ln, c + 1)
                act.activation(hms[:, c * CH:(c + 1) * CH], bank, ACT.Exp, scale=-0.5).then_inc(f_rs, 1)

            act.preload_act_table_set("natural_log_exp_and_others")
            for c in range(CHUNKS):
                for q, (m0, m1) in enumerate(LAST_TILES):
                    taken(act, G_LAST + 3 * c + q)
                    if c == 2 and q == 0:
                        act.wait_ge(f_st, 1)
                    act.activation(fsq[c][:, q, 0:(m1 - m0) * CH].rearrange("p (a n) -> p a n", a=m1 - m0),
                                   mix[:, m0:m1, c * CH:(c + 1) * CH], ACT.Square).then_inc(f_sq, 1)
                    for m in range(max(m0, YD), m1):
                        out = act.activation(fgain[:, m - YD, c * CH:(c + 1) * CH], mix[:, m, c * CH:(c + 1) * CH],
                                             ACT.Copy, scale=vec[:, V_FPOST + m:V_FPOST + m + 1])
                        if m == KT - 1:
                            out.then_inc(f_gain, 1)
                    if q == 1 and c > 0:
                        f_rms(c - 1)
            f_rms(CHUNKS - 1)

        @block.vector
        def _(dve):
            steps = [0]

            def step(instruction):
                instruction.then_inc(dve_c, 1)
                steps[0] += 1
                dve.wait_ge(dve_c, steps[0])

            dve.memset(ones[:], 1.0).then_inc(c_init, 1)
            dve.memset(eps_b[:], EPS).then_inc(c_init, 1)
            dve.memset(eps15_b[:], EPS ** 1.5).then_inc(c_init, 1)
            dve.sem_inc(s_new, 1)
            dve.sem_inc(wo_sum, 1)
            dve.sem_inc(hid_lo, 2)
            dve.sem_inc(mg_rdy, 1)
            step(dve.memset(u_ext[:, :, 0:HIST], 0.0))

            dve.wait_ge(x_ld[0], 32)
            first = xsq[:, 0, :].rearrange("p (k n) -> p k n", k=KT)
            step(dve.tensor_tensor(first[:, 4:8], x_in[:, 4:8, 0:CH], x_in[:, 4:8, 0:CH], ALU.mult))
            dve.wait_ge(x_sq, 1)
            step(dve.tensor_tensor(first[:, 0:4], first[:, 0:4], first[:, 4:8], ALU.add))
            step(dve.tensor_tensor(first[:, 0:2], first[:, 0:2], first[:, 2:4], ALU.add))
            dve.tensor_tensor(first[:, 0], first[:, 0], first[:, 1], ALU.add).then_inc(x_one, 1)

            dve.wait_ge(cst_ld, 48)
            for c in range(CHUNKS):
                cs = slice(c * CH, (c + 1) * CH)
                dve.wait_ge(x_rs, c + 1)
                for half in range(2):
                    xh = x_in[:, 4 * half:4 * half + 4, cs]
                    last = c == CHUNKS - 1 and half
                    dve.tensor_tensor(xh, xh, pch(G_XSTAT, c).unsqueeze(1).broadcast_to([P, 4, CH]), ALU.mult
                                      ).then_inc(ps_free[G_XSTAT % 2] if last else x_sc, 1)
                for k in range(KT):
                    dve.wait_ge(xn_hi, c * KT + k + 1)
                    dve.scalar_tensor_tensor(xn_l[:, k, cs], x_in[:, k, cs], vec[:, V_PRE + k:V_PRE + k + 1],
                                             xn_h[:, k, cs].bitcast(F32), ALU.mult, ALU.subtract).then_inc(xn_lo, 1)

            HALF = SEQ // 2
            cursor = [0]

            def tap(j, k, shift=0, i=None):
                for half in range(2):
                    bank = ps[:, 6 + half, :]
                    idx = k if i is None else i
                    u_ = (u_ext[:, j, k + HALF * half:k + HALF * (half + 1)] if i is None
                          else u_ext[:, j, bass.ds(i + HALF * half, HALF)])
                    w_ = wdw[:, j, k:k + 1] if i is None else wdw[:, j, bass.ds(i, 1)]
                    n = 2 * TAPS * j + half - 1
                    if i is not None or n + 2 * k > 0:
                        dve.wait_ge(cv_acc, (2 * k + n) if i is None else i * 2 + n)
                    if i is None and k == 0:
                        out = dve.tensor_scalar(bank, u_, w_, vec[:, V_BDW + j:V_BDW + j + 1], ALU.mult, ALU.add)
                    else:
                        dst = conv[:, j, HALF * half:HALF * (half + 1)] if (i is None and k == TAPS - 1) else bank
                        out = dve.scalar_tensor_tensor(dst, u_, w_, bank, ALU.mult, ALU.add)
                    out.then_inc(cv_acc, 1)

            def taps(n):
                while n > 0 and cursor[0] < TAPS * CT:
                    j, k = divmod(cursor[0], TAPS)
                    if k in (0, TAPS - 1):
                        tap(j, k)
                        took = 1
                    else:
                        took = min(n, TAPS - 1 - k)
                        with dve.Fori(k, k + took) as i:
                            tap(j, None, i=i)
                    cursor[0] += took
                    n -= took

            dve.wait_ge(wdw_ld, 16)
            dve.wait_ge(hist_ld, 16)
            for j in range(CT):
                g = G_U + 1 + 2 * j
                dve.wait_ge(mm, done(S_U + 4 * j + 3))
                taken(dve, g - 1)
                dve.tensor_tensor(t3(u_ext[:, j, HIST:HIST + T]), pset(g), t3(sgt[:]), ALU.mult
                                  ).then_inc(ps_free[g % 2], 1)
                taken(dve, g)
                dve.tensor_copy(hist[:, j, :, HIST], u_ext[:, j, HIST + SEQ:HIST + T]).then_inc(h_done, 1)
                dve.wait_ge(h_done, 2 * j + 1)
                step(dve.tensor_tensor(hprod[:], hist[:, j], wdw[:, j, :].unsqueeze(1).broadcast_to([P, DEC, TAPS]),
                                       ALU.mult))
                step(dve.reduce_sum(conv[:, j, SEQ:T], hprod[:], mybir.AxisListType.X))
                dve.tensor_scalar(conv[:, j, SEQ:T], conv[:, j, SEQ:T], vec[:, V_BDW + j:V_BDW + j + 1], None,
                                  ALU.add).then_inc(h_done, 1)
                taps((14, 14, 14, 13)[j])

            def rotate(p, w):
                taken(dve, G_QKV[p] + 2 * w)
                taken(dve, G_QKV[p] + 2 * w + 1)
                for c in range(CHUNKS):
                    cs = slice(c * CH, (c + 1) * CH)
                    first, second = vv[p][:, 2 * w, cs], vv[p][:, 2 * w + 1, cs]
                    if 2 * p + w + c > 0:
                        dve.wait_ge(rope_done, CHUNKS * (2 * p + w) + c)
                    cos, sin = rtab[p][:, 2 * w, cs], rtab[p][:, 2 * w + 1, cs]
                    for k, (a, b) in enumerate(((first, cos), (second, sin), (second, cos), (first, sin))):
                        out = dve.tensor_tensor(rtmp[p][:, k, :], a, b, ALU.mult)
                    out.then_inc(rope_p, 1)
                    dve.wait_ge(rope_p, 2 * CHUNKS * p + CHUNKS * w + c + 1)
                    for h in range(2):
                        hs = slice(64 * h, 64 * h + 64)
                        dve.tensor_tensor(qk[p][0:64, 2 * w + h, cs], rtmp[p][hs, 0, :], rtmp[p][hs, 1, :],
                                          ALU.subtract)
                        out = dve.tensor_tensor(qk[p][64:128, 2 * w + h, cs], rtmp[p][hs, 2, :], rtmp[p][hs, 3, :],
                                                ALU.add)
                    out.then_inc(rope_done, 1)

            dve.wait_ge(tab_ld[0], 16)
            dve.wait_ge(xn_hi, CHUNKS * KT)
            rotate(0, 0)
            taps(3)
            rotate(0, 1)
            taps(17)
            for t in range(4):
                g = G_G[0] + t
                dve.wait_ge(g_sg, t + 1)
                dve.tensor_tensor(t3(gbuf[:, t, :]), pset(g), t3(gbuf[:, t, :]), ALU.mult
                                  ).then_inc(ps_free[g % 2], 1)
                taps(7 if t < 3 else TAPS * CT)

            dve.wait_ge(lnm_st, 1)
            for j in range(CT):
                dve.scalar_tensor_tensor(t3(conv[:, j, :]), pset(G_LNM), -1.0 / CONV_DIM, t3(conv[:, j, :]),
                                         ALU.mult, ALU.add
                                         ).then_inc(ln_xc if j < CT - 1 else ps_free[G_LNM % 2], 1)
            dve.wait_ge(ln_rs, 1)
            for j in range(CT):
                dve.tensor_tensor(t3(conv[:, j, :]), t3(conv[:, j, :]), pset(G_LNV), ALU.mult
                                  ).then_inc(ln_n if j < CT - 1 else ps_free[G_LNV % 2], 1)
            for j in range(CT):
                dve.wait_ge(ln_sg, j + 1)
                dve.tensor_scalar(conv[:, j, :], conv[:, j, :], vec[:, V_LNW + j:V_LNW + j + 1],
                                  vec[:, V_LNB + j:V_LNB + j + 1], ALU.mult, ALU.add).then_inc(ln_z, 1)
                dve.wait_ge(ln_z, j + 1)
                dve.tensor_tensor(conv[:, j, :], conv[:, j, :], u_ext[:, j, 0:T], ALU.mult).then_inc(ln_y, 1)
            for j in range(CT):
                dve.wait_ge(cv_hi, j + 1)
                dve.tensor_tensor(cv_l[:, j, :], conv[:, j, :], cv_h[:, j, 0:T].bitcast(F32), ALU.subtract
                                  ).then_inc(cv_lo, 1)

            def chunk(p, n, b, u, loads):
                dve.wait_ge(ret_a, n + 1)
                dve.tensor_tensor(p_b[:], B6[:, 0:2 * RC].rearrange("p (h n) -> p h n", h=2),
                                  mask[:].unsqueeze(1).broadcast_to([P, 2, RC]), ALU.mult).then_inc(pk_rdy, 1)
                for h in range(2):
                    dve.tensor_scalar(kt_b[:, h, :], B6[:, (2 + h) * RC:(3 + h) * RC],
                                      float(GAMMA[2 * p + h] ** RC), None, ALU.mult).then_inc(pk_rdy, 1)
                dve.tensor_copy(qd_b[:, u % 2, :], qk[p][:, 0:2, bass.ds(b + SEQ, 1)].rearrange("p h a -> p (h a)"))
                dve.wait_ge(ss_ld[u % 2], loads)
                dve.wait_ge(vb_ld, n * 16 + 16)
                for h in range(2):
                    hs = slice(h * DV, (h + 1) * DV)
                    dve.tensor_scalar(v_bc[:, hs], v_bc[:, hs], qk[p][:, 2 + h, bass.ds(b + SEQ, 1)], None,
                                      ALU.mult).then_inc(s_kv, 1)
                dve.wait_ge(s_kv, n * 2 + 2)
                for h in range(2):
                    hs = slice(h * DV, (h + 1) * DV)
                    out = dve.scalar_tensor_tensor(s_dec[:, u % 2, hs], s_dec[:, u % 2, hs], float(GAMMA[2 * p + h]),
                                                   v_bc[:, hs], ALU.mult, ALU.add)
                out.then_inc(s_new, 1)
                dve.wait_ge(ret_b, n + 2)
                dve.wait_ge(s_upd, n + (p + 1))
                for h in range(2):
                    out = dve.scalar_tensor_tensor(state[:, h, :], state[:, h, :], float(GAMMA[2 * p + h] ** RC),
                                                   B7[:, h * DV:(h + 1) * DV], ALU.mult, ALU.add)
                out.then_inc(s_upd, 1)

            def normed_outputs(p):
                def norm(i):
                    h, c = divmod(i, CHUNKS)
                    dve.wait_ge(on_rs, 6 * p + i + 1)
                    o = vv[p][:, 2 * h:2 * h + 2, c * CH:(c + 1) * CH]
                    dve.tensor_tensor(o, o, ps[:, 6 + i % 2, 0:CH].unsqueeze(1).broadcast_to([P, 2, CH]), ALU.mult
                                      ).then_inc(on_n, 1)

                def gate(t):
                    dve.tensor_tensor(vv[p][:, t, :], vv[p][:, t, :], gbuf[:, t, :], ALU.mult).then_inc(ro_g, 1)

                def low(t):
                    dve.wait_ge(ro_hi, 4 * p + t + 1)
                    dve.tensor_tensor(ro_l[p][:, t, :], vv[p][:, t, :], ro_h[p][:, t, :].bitcast(F32), ALU.subtract
                                      ).then_inc(ro_lo, 1)

                for h in range(2):
                    for c in range(CHUNKS):
                        norm(3 * h + c)
                    dve.wait_ge(on_n, 6 * p + 3 * h + 3)
                    gate(2 * h)
                    gate(2 * h + 1)
                for t in range(4):
                    low(t)

            dve.memset(state[:], 0.0).then_inc(s_upd, 1)
            dve.wait_ge(cst_ld, 48)
            taken(dve, G_LNV + 2)
            taken(dve, G_LNV + 3)
            with dve.Fori(0, NRC // 2) as i:
                for u in range(2):
                    c = i * 2 + u
                    g = G_AOUT + u
                    chunk(0, c, c, u, i * 16 + 16)
                    dve.wait_ge(mm, i * 2 + done(S_AOUT + u))
                    dve.tensor_copy(v0[:, :, bass.ds(c + SEQ, 1)].rearrange("p t a -> p (t a)"),
                                    ps[:, 3 * (g % 2), CH + 8:CH + 12])
                    tile_ = t3(ma[:, bass.ds(c, 1), :].rearrange("p a n -> p (a n)"))
                    dve.tensor_tensor(tile_, pset(g), tile_, ALU.mult).then_inc(ps_free[g % 2], 1)
            normed_outputs(0)

            dve.wait_ge(tab_ld[1], 16)
            rotate(1, 0)
            rotate(1, 1)
            dve.wait_ge(rp_st, 16)
            dve.memset(state[:], 0.0).then_inc(s_upd, 1)
            with dve.Fori(0, NRC // 4) as i:
                for u in range(4):
                    c = i * 4 + u
                    chunk(1, c + NRC, c, u, i * 32 + (16 * (u // 2) + 16 + 16 * (DEC // 2)))
                    if u % 2:
                        t = u // 2
                        g = G_G[1] + t
                        dve.wait_ge(g_sg, i * 2 + (5 + t))
                        dve.tensor_copy(v1[:, :, bass.ds(c + (SEQ - 1), 2)],
                                        ps[:, 3 * (g % 2), CH + 8:CH + 16].rearrange("p (b t) -> p t b", b=2))
                        tile_ = t3(gbuf[:, bass.ds(i * 2 + t, 1), :].rearrange("p a n -> p (a n)"))
                        dve.tensor_tensor(tile_, pset(g), tile_, ALU.mult).then_inc(ps_free[g % 2], 1)
            normed_outputs(1)

            def merge(m, gs, ss):
                g = G_GB + 1
                dve.wait_ge(mm, ss + done(S_GB + 3))
                taken(dve, G_GB, gs)
                dve.wait_ge(mg_rdy, m + 1)
                dve.tensor_tensor(t3(gbuf[:, 1, :]), pset(g), t3(gbuf[:, 0, :]), ALU.mult
                                  ).then_inc(ps_free[g % 2], 1)
                taken(dve, g, gs)
                tile_ = ma[:, bass.ds(m, 1), :].rearrange("p a n -> p (a n)")
                dve.tensor_tensor(tile_, tile_, gbuf[:, 1, :], ALU.add).then_inc(mg_rdy, 1)

            def merged_lo(m):
                dve.wait_ge(mg_hi, m + 1)
                dve.tensor_tensor(mg_l[:, m, :], ma[:, m, :], mg_h[:, m, :].bitcast(F32), ALU.subtract
                                  ).then_inc(mg_lo, 1)

            with dve.Fori(0, KT - 1) as i:
                merge(i, i, i * 4)
            for m in range(KT - 1):
                merged_lo(m)
            merge(KT - 1, KT - 1, 4 * (KT - 1))
            merged_lo(KT - 1)

            dve.memset(gbuf[:, 3, :], 0.0).then_inc(wo_sum, 1)
            with dve.Fori(0, 2) as i:
                for u in range(2):
                    dve.wait_ge(wo_sq, i * 2 + (u + 1))
                    dve.wait_ge(wo_sum, i * 2 + (u + 2))
                    dve.tensor_tensor(gbuf[:, 3, :], gbuf[:, 3, :], gbuf[:, 1 + u, :], ALU.add).then_inc(wo_sum, 1)

            def wob_sum(c, half):
                dve.wait_ge(wo_sq, 4 + 2 * c + half + 1)
                for m in range(2):
                    dve.wait_ge(wo_sum, 6 + 4 * c + 2 * half + m)
                    dve.tensor_tensor(gbuf[:, 3, c * CH:(c + 1) * CH], gbuf[:, 3, c * CH:(c + 1) * CH],
                                      gbuf[:, 1 + half, m * CH:(m + 1) * CH], ALU.add).then_inc(wo_sum, 1)

            def m_norm(c):
                cs = slice(c * CH, (c + 1) * CH)
                dve.wait_ge(m_rs, c + 1)
                for half in (1, 0):
                    t = mix[:, 4 * half:4 * half + 4, cs]
                    dve.tensor_tensor(t, t, ps[:, 6 + c % 2, 0:CH].unsqueeze(1).broadcast_to([P, 4, CH]), ALU.mult
                                      ).then_inc(m_sc, 1)
                dve.wait_ge(m_sc, 2 * c + 2)
                dve.tensor_tensor(h_res[:, 0:4, cs], mix[:, 0:4, cs], h_res[:, 0:4, cs], ALU.add).then_inc(h_dve, 1)

            def fx_lo_part(c):
                cs = slice(c * CH, (c + 1) * CH)
                for k in range(KT):
                    dve.wait_ge(fx_hi, c * KT + k + 1)
                    dve.scalar_tensor_tensor(fx_l[:, k, cs], h_res[:, k, cs], vec[:, V_FPRE + k:V_FPRE + k + 1],
                                             fx_h[:, k, cs].bitcast(F32), ALU.mult, ALU.subtract).then_inc(fx_lo, 1)

            wob_sum(0, 0)
            wob_sum(0, 1)
            wob_sum(1, 0)
            dve.wait_ge(xa_ld, 16)
            m_norm(0)
            wob_sum(1, 1)
            wob_sum(2, 0)
            m_norm(1)
            wob_sum(2, 1)
            fx_lo_part(0)
            fx_lo_part(1)
            m_norm(2)
            fx_lo_part(2)
            dve.memset(hsum[:], 0.0).then_inc(h_sum, 1)
            dve.wait_ge(h_pool, CHUNKS)
            dve.memset(mix[:], 0.0).then_inc(f_zero, 1)
            dve.wait_ge(f_zero, 1)

            def hidden_lo(b, j, n):
                dve.wait_ge(hid_hi, n + 1)
                dve.tensor_tensor(hid_l[:, FB * (b % 2) + j, :], gbuf[:, 2 + j, :],
                                  hid_h[:, FB * (b % 2) + j, :].bitcast(F32), ALU.subtract).then_inc(hid_lo, 1)

            def add_down(m, g, ev, gshift=0):
                dve.wait_ge(mm, ev)
                taken(dve, g - 2, gshift)
                dve.tensor_tensor(t3(mix[:, m, :]), pset(g), t3(mix[:, m, :]), ALU.add
                                  ).then_inc(ps_free[g % 2], 1)

            def block_out(b, gs=0, es=0, hs=0):
                hidden_lo(b + 1, 0, hs + 2 * (b + 1))
                for m in range(KT):
                    if m == 1:
                        hidden_lo(b + 1, 1, hs + (2 * (b + 1) + 1))
                    add_down(m, G_FFN + 4 + 10 * b + m, es + (E_FFN + PER_FB * b + 4 + m + 1), gs)

            for j in range(FB):
                hidden_lo(0, j, j)
            with dve.Fori(0, (NFB - 2) // 2) as i:
                block_out(0, i * 10, i * (2 * PER_FB), i * 4)
                block_out(1, i * 10, i * (2 * PER_FB), i * 4)
                dve.wait_ge(h_sq, i + 1)
                dve.wait_ge(h_sum, i + 1)
                dve.tensor_tensor(hsum[:], hsum[:], hsq[:], ALU.add).then_inc(h_sum, 1)
            dve.wait_ge(h_sq, KT)
            dve.wait_ge(h_sum, KT)
            dve.tensor_tensor(hsum[:], hsum[:], hsq[:], ALU.add).then_inc(h_sum, 1)
            block_out(NFB - 2)

            def last_down(c, q):
                m0, m1 = LAST_TILES[q]
                g = G_LAST + 3 * c + q
                dve.wait_ge(mm, E_LAST + 3 * c + q + 1)
                taken(dve, g - 2)
                t = mix[:, m0:m1, c * CH:(c + 1) * CH]
                dve.tensor_tensor(t, ps[:, 3 * (g % 2):3 * (g % 2) + m1 - m0, 0:CH], t, ALU.add
                                  ).then_inc(ps_free[g % 2], 1)

            def root_argument(c):
                bank = ps[:, 6 + c % 2, 0:CH]
                dve.wait_ge(f_st, c + 1)
                dve.wait_ge(h_cp, c + 1)
                dve.scalar_tensor_tensor(bank, bank, 1.0 / D_MODEL, hms[:, c * CH:(c + 1) * CH],
                                         ALU.mult, ALU.add).then_inc(f_den, 1)

            def out_norm(c):
                cs = slice(c * CH, (c + 1) * CH)
                dve.wait_ge(f_rs, c + 1)
                for k in range(YD):
                    out = dve.scalar_tensor_tensor(mix[:, k, cs], mix[:, k, cs], vec[:, V_FPOST + k:V_FPOST + k + 1],
                                                   hms[:, cs], ALU.mult, ALU.mult)
                out.then_inc(y_sc, 1)

            def out_residual(c):
                cs = slice(c * CH, (c + 1) * CH)
                dve.wait_ge(y_sc, c + 1)
                dve.tensor_tensor(h_res[:, 0:YD, cs], mix[:, 0:YD, cs], h_res[:, 0:YD, cs], ALU.add).then_inc(y_dve, 1)

            for q in range(3):
                last_down(0, q)
            last_down(1, 0)
            last_down(1, 1)
            root_argument(0)
            last_down(1, 2)
            out_norm(0)
            out_residual(0)
            last_down(2, 0)
            last_down(2, 1)
            root_argument(1)
            dve.wait_ge(f_sq, 8)
            dve.tensor_tensor(fsqA[:, 0, :], fsqA[:, 0, :], fsqA[:, 1, :], ALU.add).then_inc(f_sum, 1)
            last_down(2, 2)
            out_norm(1)
            root_argument(2)
            out_residual(1)
            out_norm(2)
            out_residual(2)


def rope_tables():
    half = DK // 2
    steps = np.linspace(0.0, 1.0, half, dtype=np.float32).astype(np.float64)
    freqs = np.float32(1.0) / (ROPE_BASE ** steps).astype(np.float32)
    pos = np.concatenate([np.arange(SEQ), np.full(DEC, PAST_LEN)]).astype(np.float32)
    ang = (pos[None, :] * freqs[:, None]).astype(np.float32).astype(np.float64)
    place = np.where(np.arange(T) < SEQ, np.arange(T) % RC + 1, 0)
    out = np.empty((PAIRS, 2, half, 4, T), np.float64)
    for p in range(PAIRS):
        for h in range(2):
            decay = GAMMA[2 * p + h] ** place
            for w, factor in enumerate((decay, DK ** -0.5 / decay)):
                out[p, h, :, 2 * w] = np.cos(ang) * factor
                out[p, h, :, 2 * w + 1] = np.sin(ang) * factor
    return out.reshape(PAIRS, P, 4, T).astype(np.float32)


def weight_stream(w_in, w_conv, w_ret, w_o, w_up, w_down):
    n_val, n_gate, n_q, n_k = 0, CONV_DIM, 2 * CONV_DIM, 2 * CONV_DIM + HEADS * DK
    n_v = n_k + HEADS * DK
    n_g = n_v + HEADS * DV
    n_ga = n_g + HEADS * DV
    n_gb = n_ga + D_MODEL
    slots = []

    def put(w, ks, cols):
        slots.append(np.stack([w[k * P:(k + 1) * P, cols] for k in ks], axis=1))

    def put8(w, cols):
        put(w, range(4), cols)
        put(w, range(4, 8), cols)

    def run(start):
        return np.arange(start, start + P)

    for j in range(CT):
        put8(w_in, run(n_gate + j * P))
        put8(w_in, run(n_val + j * P))

    def qkv(p):
        half = DK // 2
        for base in (n_q, n_k):
            for part in range(2):
                put8(w_in, np.concatenate([base + (2 * p + h) * DK + part * half + np.arange(half) for h in range(2)]))
        for t in range(4):
            put8(w_in, run(n_v + (4 * p + t) * P))

    def gate(p):
        for t in range(4):
            put8(w_in, run(n_g + (4 * p + t) * P))

    qkv(0)
    gate(0)
    for m in range(KT):
        put8(w_in, run(n_ga + m * P))
    for m in range(KT):
        put(w_conv, range(4), run(m * P))
    qkv(1)
    gate(1)
    for m in range(KT):
        put8(w_in, run(n_gb + m * P))
        put8(w_ret, run(m * P))
    for m in range(KT):
        put8(w_o, run(m * P))

    def up(b):
        for j in range(FB):
            put8(w_up, run((FB * b + j) * P))

    def down(b):
        for m in range(0, KT, 2):
            slots.append(np.stack([w_down[(FB * b + k) * P:(FB * b + k + 1) * P, run((m + a) * P)]
                                   for a in range(2) for k in range(FB)], axis=1))

    up(0)
    for b in range(NFB):
        if b + 1 < NFB:
            up(b + 1)
        down(b)
    assert len(slots) == NSLOT
    return np.ascontiguousarray(np.stack(slots).reshape(NSLOT, P, SLOT))


def kernel(x_prompt, x_sample, cache_conv, state_ret, norm_mix_pre, norm_mix_post, w_in, w_dw, b_dw,
           conv_ln_w, conv_ln_b, w_conv_out, w_ret_out, w_o, norm_ffn_pre, norm_ffn_post, w_ffn_up,
           w_ffn_down):
    import concourse.bacc as bacc
    from concourse.bass_utils import run_bass_kernel_spmd

    def a(x):
        return np.asarray(x)

    x = np.concatenate([a(x_prompt)[0], a(x_sample)[:, 0]], axis=0)
    cols = [a(v)[0].reshape(-1, P).T for v in (norm_mix_pre, norm_mix_post, norm_ffn_pre, norm_ffn_post,
                                               conv_ln_w, conv_ln_b, b_dw)]
    history = np.zeros((P, CT, DEC, TAPS), np.float32)
    history[..., :HIST] = a(cache_conv)[0].reshape(DEC, HIST, CT, P).transpose(3, 2, 0, 1)
    ins = {
        "xT": x.T.reshape(KT, P, T).transpose(1, 0, 2),
        "wseq": weight_stream(a(w_in)[0], a(w_conv_out)[0], a(w_ret_out)[0], a(w_o)[0], a(w_ffn_up)[0],
                              a(w_ffn_down)[0]),
        "vecs": np.concatenate(cols, axis=1),
        "wdwT": a(w_dw)[0].reshape(TAPS, CT, P).transpose(2, 1, 0),
        "cacheT": history,
        "s_in": a(state_ret)[0],
        "rope": rope_tables(),
        "mask": np.triu(np.ones((RC, RC), np.float32)),
        "ident_in": np.eye(P, dtype=np.float32),
    }
    outs = {
        "yT": (P, KT, T),
        "convp": (P, CT, HIST),
        "convs": (P, CT, DEC, TAPS),
        "retp": (HEADS, DK, DV),
        "rets": (DEC, HEADS, DK, DV),
    }
    nc = bacc.Bacc("TRN2", target_bir_lowering=False, num_devices=1)
    ins = {name: np.ascontiguousarray(v) for name, v in ins.items()}
    args = [nc.dram_tensor(f"{name}_dram", v.shape, mybir.dt.from_np(v.dtype), kind="ExternalInput").ap()
            for name, v in ins.items()]
    args += [nc.dram_tensor(f"{name}_dram", shape, F32, kind="ExternalOutput").ap() for name, shape in outs.items()]
    build(nc, *args)
    r = run_bass_kernel_spmd(nc, [{f"{name}_dram": v for name, v in ins.items()}], core_ids=[0]).results[0]
    got = {name: np.asarray(r[f"{name}_dram"]) for name in outs}
    y = got["yT"].transpose(2, 1, 0).reshape(T, D_MODEL)
    return (y[:SEQ][None], y[SEQ:][:, None],
            got["convp"].transpose(2, 1, 0).reshape(1, 1, HIST, CONV_DIM),
            got["retp"][None, None],
            got["convs"][..., 1:].transpose(2, 3, 1, 0).reshape(1, DEC, HIST, CONV_DIM),
            got["rets"][None])
```
